# Optimizing a Trainium2 kernel written in Bass

```python
import math
import jax, jax.numpy as jnp
from jax import lax
import numpy as np

D_MODEL = 1024
BATCH = 1
SEQ = 256
DEPTH = 1
DEC_BATCH = 8
DEC_SEQ = 1
PAST_LEN = 1024
PAGE_SIZE = 128

CONV_WIDTH = D_MODEL // 4
CONV_K = 3
ATTN_HEAD_DIM = 64
ATTN_HEADS = (D_MODEL - CONV_WIDTH) // ATTN_HEAD_DIM
ATTN_WIDTH = ATTN_HEADS * ATTN_HEAD_DIM
D_MIX = CONV_WIDTH + ATTN_WIDTH
D_IN_PROJ = 3 * CONV_WIDTH + 3 * ATTN_WIDTH
DILATED_PATTERNS = ((128, 1), (512, 4), (2048, 16))
WINDOW_MAX = max(w for w, _ in DILATED_PATTERNS)
ATTN_SCALE = 1.0 / math.sqrt(ATTN_HEAD_DIM)
N_BUCKETS = 32
MAX_DISTANCE = WINDOW_MAX
MEM_TOKENS = 256
MEM_HEADS = 4
MEM_HEAD_DIM = D_MODEL // MEM_HEADS
MEM_WIDTH = MEM_HEADS * MEM_HEAD_DIM
MEM_SCALE = 1.0 / math.sqrt(MEM_HEAD_DIM)
N_EXPERTS = 32
TOP_K = 4
D_FF = D_MODEL
SWIGLU_LIMIT = 7.0
SWIGLU_ALPHA = 1.702
EXPERT_BLOCK = 128
LN_EPS = 1e-5
DEEPNORM_ALPHA = (2 * DEPTH) ** 0.25
DEEPNORM_BETA = (8 * DEPTH) ** -0.25
NEG_INF = -1e30

kernel_name = 'hymba_conv_dilated_attn_moe_decoder_step'

def layer_norm(x, g, b):
    xf = x.astype(jnp.float32)
    mu = jnp.mean(xf, axis=-1, keepdims=True)
    var = jnp.mean(jnp.square(xf - mu), axis=-1, keepdims=True)
    return ((xf - mu) * lax.rsqrt(var + LN_EPS) * g.astype(jnp.float32) + b.astype(jnp.float32)).astype(x.dtype)

def rel_bucket(dist):
    max_exact = N_BUCKETS // 2
    df = jnp.maximum(dist, 1).astype(jnp.float32)
    large = max_exact + (jnp.log(df / max_exact) / math.log(MAX_DISTANCE / max_exact)
                         * (N_BUCKETS - max_exact)).astype(jnp.int32)
    return jnp.where(dist < max_exact, dist, jnp.minimum(large, N_BUCKETS - 1))

def masked_softmax(logits, valid):
    logits = jnp.where(valid, logits, NEG_INF)
    m = jnp.max(logits, axis=-1, keepdims=True)
    p = jnp.exp(logits - m)
    s = jnp.sum(p, axis=-1, keepdims=True)
    return p / s, (m + jnp.log(s))[..., 0]

def combine_dilations(outs, lses):
    w = jax.nn.softmax(jnp.stack(lses, axis=0), axis=0)
    return jnp.einsum('pbsh,pbshe->bshe', w.astype(outs[0].dtype), jnp.stack(outs, axis=0))

def split_projection(x, w_in):
    proj = x @ w_in
    gb, gc, h, q, k, v = jnp.split(
        proj, [CONV_WIDTH, 2 * CONV_WIDTH, 3 * CONV_WIDTH,
               3 * CONV_WIDTH + ATTN_WIDTH, 3 * CONV_WIDTH + 2 * ATTN_WIDTH], axis=-1)
    heads = lambda t: t.reshape(t.shape[0], t.shape[1], ATTN_HEADS, ATTN_HEAD_DIM)
    return gb, gc * h, heads(q), heads(k), heads(v)

def short_conv(u_pad, w_conv):
    S = u_pad.shape[1] - (CONV_K - 1)
    out = w_conv[0] * u_pad[:, :S]
    for i in range(1, CONV_K):
        out = out + w_conv[i] * u_pad[:, i:i + S]
    return out

def dilated_attention_prompt(q, k, v, rel_table):
    B, S, H, E = q.shape
    outs, lses = [], []
    for window, dil in DILATED_PATTERNS:
        n = window // dil
        L = S // dil
        nb = -(-L // n)
        Lq = nb * n

        def classes(t, front):
            t = t.reshape(B, L, dil, H, E)
            return jnp.pad(t, ((0, 0), (front, Lq - L), (0, 0), (0, 0), (0, 0)))

        qb = classes(q, 0).reshape(B, nb, n, dil, H, E)
        kp, vp = classes(k, n), classes(v, n)
        kb = jnp.concatenate([kp[:, :Lq].reshape(B, nb, n, dil, H, E),
                              kp[:, n:].reshape(B, nb, n, dil, H, E)], axis=2)
        vb = jnp.concatenate([vp[:, :Lq].reshape(B, nb, n, dil, H, E),
                              vp[:, n:].reshape(B, nb, n, dil, H, E)], axis=2)
        qi = jnp.arange(n)[:, None]
        kj = jnp.arange(2 * n)[None, :]
        dist = qi - kj + n
        key_sub = jnp.arange(nb)[:, None, None] * n + kj - n
        valid = (dist >= 0) & (dist <= n) & (key_sub >= 0)
        bias = rel_table[rel_bucket(jnp.clip(dist, 0, n) * dil)].astype(jnp.float32)
        logits = jnp.einsum('bnqrhe,bnkrhe->bnrhqk', qb, kb).astype(jnp.float32) * ATTN_SCALE
        logits = logits + jnp.transpose(bias, (2, 0, 1))
        probs, lse = masked_softmax(logits, valid[:, None, None])
        o = jnp.einsum('bnrhqk,bnkrhe->bnqrhe', probs.astype(vb.dtype), vb)
        outs.append(o.reshape(B, Lq, dil, H, E)[:, :L].reshape(B, S, H, E))
        lses.append(jnp.transpose(lse, (0, 1, 4, 2, 3)).reshape(B, Lq, dil, H)[:, :L].reshape(B, S, H))
    return combine_dilations(outs, lses)

def dilated_attention_sample(q, k_new, v_new, win_k, win_v, rel_table):
    DB, DS, H, E = q.shape
    W = win_k.shape[1]
    k_all = jnp.concatenate([win_k, k_new], axis=1)
    v_all = jnp.concatenate([win_v, v_new], axis=1)
    pos_q = PAST_LEN + jnp.arange(DS)
    outs, lses = [], []
    for window, dil in DILATED_PATTERNS:
        n = window // dil
        taps = jnp.arange(n + 1)
        pos_k = pos_q[:, None] - taps[None, :] * dil
        idx = jnp.where(pos_k < PAST_LEN, jnp.mod(pos_k, W), W + pos_k - PAST_LEN)
        kg = k_all[:, idx]
        vg = v_all[:, idx]
        bias = rel_table[rel_bucket(taps * dil)].astype(jnp.float32)
        logits = jnp.einsum('bqhe,bqjhe->bhqj', q, kg).astype(jnp.float32) * ATTN_SCALE
        logits = logits + jnp.transpose(bias)[:, None, :]
        probs, lse = masked_softmax(logits, (pos_k >= 0)[None, None])
        outs.append(jnp.einsum('bhqj,bqjhe->bqhe', probs.astype(vg.dtype), vg))
        lses.append(jnp.transpose(lse, (0, 2, 1)))
    return combine_dilations(outs, lses)

def memory_attention(x, mem_k, mem_v, w_q, w_o):
    B, S, _ = x.shape
    q = (x @ w_q).reshape(B, S, MEM_HEADS, MEM_HEAD_DIM)
    logits = jnp.einsum('bshe,bmhe->bhsm', q, mem_k).astype(jnp.float32) * MEM_SCALE
    probs = jax.nn.softmax(logits, axis=-1)
    o = jnp.einsum('bhsm,bmhe->bshe', probs.astype(mem_v.dtype), mem_v).reshape(B, S, MEM_WIDTH)
    return o @ w_o

def moe_ffn(x, w_router, b_router, w_gate_up, b_gate_up, w_down, b_down):
    lead = x.shape[:-1]
    xf = x.reshape(-1, D_MODEL)
    T = xf.shape[0]
    A = T * TOP_K
    logits = (xf @ w_router + b_router).astype(jnp.float32)
    top_logit, top_idx = lax.top_k(logits, TOP_K)
    gates = jax.nn.softmax(top_logit, axis=-1)
    a_exp = top_idx.reshape(A)
    a_tok = jnp.arange(A, dtype=jnp.int32) // TOP_K
    order = jnp.argsort(a_exp)
    s_exp = a_exp[order]
    counts = jnp.bincount(a_exp, length=N_EXPERTS)
    starts = jnp.cumsum(counts) - counts
    padded = (counts + EXPERT_BLOCK - 1) // EXPERT_BLOCK * EXPERT_BLOCK
    pends = jnp.cumsum(padded)
    pstarts = pends - padded
    dest = pstarts[s_exp] + jnp.arange(A, dtype=jnp.int32) - starts[s_exp]
    n_blocks = A // EXPERT_BLOCK + N_EXPERTS
    P = n_blocks * EXPERT_BLOCK
    buf_tok = jnp.full((P,), T, jnp.int32).at[dest].set(a_tok[order])
    buf_gate = jnp.zeros((P,), jnp.float32).at[dest].set(gates.reshape(A)[order])
    blk_exp = jnp.minimum(jnp.searchsorted(pends, jnp.arange(n_blocks, dtype=jnp.int32) * EXPERT_BLOCK,
                                           side='right'), N_EXPERTS - 1)
    xb = jnp.concatenate([xf, jnp.zeros((1, D_MODEL), xf.dtype)], axis=0)[buf_tok]
    xb = xb.reshape(n_blocks, EXPERT_BLOCK, D_MODEL)

    def expert_block(args):
        xblk, e = args
        gu = xblk @ w_gate_up[e] + b_gate_up[e]
        g, u = jnp.split(gu, 2, axis=-1)
        g = jnp.minimum(g, SWIGLU_LIMIT)
        u = jnp.clip(u, -SWIGLU_LIMIT, SWIGLU_LIMIT)
        act = (u + 1.0) * g * jax.nn.sigmoid(SWIGLU_ALPHA * g)
        return act @ w_down[e] + b_down[e]

    yb = lax.map(expert_block, (xb, blk_exp)).reshape(P, D_MODEL)
    y = jnp.zeros((T + 1, D_MODEL), yb.dtype).at[buf_tok].add(yb * buf_gate[:, None].astype(yb.dtype))
    return y[:T].reshape(*lead, D_MODEL)

def layer_tail(x, mixed, mem_k, mem_v, w_out, ln1_g, ln1_b, w_mem_q, w_mem_o, ln2_g, ln2_b,
               w_router, b_router, w_gate_up, b_gate_up, w_down, b_down, ln3_g, ln3_b):
    x = layer_norm(DEEPNORM_ALPHA * x + mixed @ w_out, ln1_g, ln1_b)
    x = layer_norm(DEEPNORM_ALPHA * x + memory_attention(x, mem_k, mem_v, w_mem_q, w_mem_o), ln2_g, ln2_b)
    x = layer_norm(DEEPNORM_ALPHA * x + moe_ffn(x, w_router, b_router, w_gate_up, b_gate_up, w_down, b_down),
                   ln3_g, ln3_b)
    return x

def setup_inputs(seed: int = 0) -> dict:
    key = jax.random.key(seed)
    ks = iter(jax.random.split(key, 32))

    def nrm(shape, scale):
        return scale * jax.random.normal(next(ks), shape, jnp.float32)

    win_s = min(WINDOW_MAX, PAST_LEN)
    return {
        'x_prompt': nrm((BATCH, SEQ, D_MODEL), 1.0),
        'x_sample': nrm((DEC_BATCH, DEC_SEQ, D_MODEL), 1.0),
        'mem_prompt': nrm((BATCH, MEM_TOKENS, D_MODEL), 1.0),
        'cache_win_k': nrm((DEPTH, DEC_BATCH, win_s, ATTN_HEADS, ATTN_HEAD_DIM), 1.0),
        'cache_win_v': nrm((DEPTH, DEC_BATCH, win_s, ATTN_HEADS, ATTN_HEAD_DIM), 1.0),
        'state_conv': nrm((DEPTH, DEC_BATCH, CONV_K - 1, CONV_WIDTH), 1.0),
        'cache_mem_k': nrm((DEPTH, DEC_BATCH, MEM_TOKENS, MEM_HEADS, MEM_HEAD_DIM), 1.0),
        'cache_mem_v': nrm((DEPTH, DEC_BATCH, MEM_TOKENS, MEM_HEADS, MEM_HEAD_DIM), 1.0),
        'rel_bias_table': nrm((N_BUCKETS, ATTN_HEADS), 0.2),
        'w_in': nrm((DEPTH, D_MODEL, D_IN_PROJ), D_MODEL ** -0.5),
        'w_conv': nrm((DEPTH, CONV_K, CONV_WIDTH), CONV_K ** -0.5),
        'w_out': nrm((DEPTH, D_MIX, D_MODEL), DEEPNORM_BETA * D_MIX ** -0.5),
        'ln1_g': 1.0 + nrm((DEPTH, D_MODEL), 0.02),
        'ln1_b': nrm((DEPTH, D_MODEL), 0.02),
        'w_mem_q': nrm((DEPTH, D_MODEL, MEM_WIDTH), D_MODEL ** -0.5),
        'w_mem_k': nrm((DEPTH, D_MODEL, MEM_WIDTH), D_MODEL ** -0.5),
        'w_mem_v': nrm((DEPTH, D_MODEL, MEM_WIDTH), D_MODEL ** -0.5),
        'w_mem_o': nrm((DEPTH, MEM_WIDTH, D_MODEL), DEEPNORM_BETA * MEM_WIDTH ** -0.5),
        'ln2_g': 1.0 + nrm((DEPTH, D_MODEL), 0.02),
        'ln2_b': nrm((DEPTH, D_MODEL), 0.02),
        'w_router': nrm((DEPTH, D_MODEL, N_EXPERTS), D_MODEL ** -0.5),
        'b_router': nrm((DEPTH, N_EXPERTS), 0.01),
        'w_gate_up': nrm((DEPTH, N_EXPERTS, D_MODEL, 2 * D_FF), D_MODEL ** -0.5),
        'b_gate_up': nrm((DEPTH, N_EXPERTS, 2 * D_FF), 0.01),
        'w_down': nrm((DEPTH, N_EXPERTS, D_FF, D_MODEL), DEEPNORM_BETA * D_FF ** -0.5),
        'b_down': nrm((DEPTH, N_EXPERTS, D_MODEL), 0.01),
        'ln3_g': 1.0 + nrm((DEPTH, D_MODEL), 0.02),
        'ln3_b': nrm((DEPTH, D_MODEL), 0.02),
    }

def reference(x_prompt, x_sample, mem_prompt, cache_win_k, cache_win_v, state_conv, cache_mem_k, cache_mem_v,
              rel_bias_table, w_in, w_conv, w_out, ln1_g, ln1_b, w_mem_q, w_mem_k, w_mem_v, w_mem_o,
              ln2_g, ln2_b, w_router, b_router, w_gate_up, b_gate_up, w_down, b_down, ln3_g, ln3_b):
    y_p, y_s = x_prompt, x_sample
    B, S = x_prompt.shape[0], x_prompt.shape[1]
    DB, DS = x_sample.shape[0], x_sample.shape[1]
    win_p = min(WINDOW_MAX, S)
    pk, pv, pc, pmk, pmv, sk, sv, sc = [], [], [], [], [], [], [], []
    for l in range(DEPTH):
        tail_w = (w_out[l], ln1_g[l], ln1_b[l], w_mem_q[l], w_mem_o[l], ln2_g[l], ln2_b[l],
                  w_router[l], b_router[l], w_gate_up[l], b_gate_up[l], w_down[l], b_down[l], ln3_g[l], ln3_b[l])

        gb, u, q, k, v = split_projection(y_p, w_in[l])
        u_pad = jnp.pad(u, ((0, 0), (CONV_K - 1, 0), (0, 0)))
        conv_out = gb * short_conv(u_pad, w_conv[l])
        attn_out = dilated_attention_prompt(q, k, v, rel_bias_table).reshape(B, S, ATTN_WIDTH)
        mem_k = (mem_prompt @ w_mem_k[l]).reshape(B, MEM_TOKENS, MEM_HEADS, MEM_HEAD_DIM)
        mem_v = (mem_prompt @ w_mem_v[l]).reshape(B, MEM_TOKENS, MEM_HEADS, MEM_HEAD_DIM)
        pk.append(jnp.roll(k[:, S - win_p:], S % win_p, axis=1))
        pv.append(jnp.roll(v[:, S - win_p:], S % win_p, axis=1))
        pc.append(u_pad[:, -(CONV_K - 1):])
        pmk.append(mem_k)
        pmv.append(mem_v)
        y_p = layer_tail(y_p, jnp.concatenate([conv_out, attn_out], axis=-1), mem_k, mem_v, *tail_w)

        gb, u, q, k, v = split_projection(y_s, w_in[l])
        u_pad = jnp.concatenate([state_conv[l].astype(u.dtype), u], axis=1)
        conv_out = gb * short_conv(u_pad, w_conv[l])
        attn_out = dilated_attention_sample(q, k, v, cache_win_k[l], cache_win_v[l],
                                            rel_bias_table).reshape(DB, DS, ATTN_WIDTH)
        sk.append(k)
        sv.append(v)
        sc.append(u_pad[:, -(CONV_K - 1):])
        y_s = layer_tail(y_s, jnp.concatenate([conv_out, attn_out], axis=-1), cache_mem_k[l], cache_mem_v[l],
                         *tail_w)

    return (y_p, y_s, jnp.stack(pk), jnp.stack(pv), jnp.stack(pc), jnp.stack(pmk), jnp.stack(pmv),
            jnp.stack(sk), jnp.stack(sv), jnp.stack(sc))


_drawn_inputs = setup_inputs


def setup_inputs(seed=0):
    import zlib

    import numpy as np

    out = dict(_drawn_inputs(seed))
    spreads = {}
    factors = {'b_gate_up': 8.0, 'b_down': 8.0, 'ln3_g': 2.802, 'ln3_b': 3.117}
    for name, (base, spread) in spreads.items():
        noise = np.random.default_rng([zlib.crc32(name.encode()), seed]).standard_normal(out[name].shape)
        drawn = base * np.exp(spread * noise) if base else spread * noise
        out[name] = __import__('jax').numpy.asarray(drawn.astype(out[name].dtype))
    for name, factor in factors.items():
        out[name] = (out[name] * factor).astype(out[name].dtype)
    return out
```

```python
import math
from contextlib import ExitStack

import numpy as np

import concourse.bass as bass
from concourse import mybir

F32 = mybir.dt.float32
BF16 = mybir.dt.bfloat16
I32 = mybir.dt.int32
ALU = mybir.AluOpType
ACT = mybir.ActivationFunctionType
AX = mybir.AxisListType

P = 128
D = 1024
DC = D // P
NP_ = 256
NS = 8
T = NP_ + NS
TCH = [(0, P), (P, P), (2 * P, NS)]
CW = 256
H = 12
E = 64
AW = H * E
HP = H // 2
NPROJ = 3 * CW + 3 * AW
MH = 4
MT = 256
NX = 32
TOPK = 4
SLOTS = 64
EPS = 1e-5
ALPHA = 2 ** 0.25
PAST = 1024
PATTERNS = ((128, 1), (512, 4), (2048, 16))
NEG = -1e30
RING = 12
ROWB = (4, 6, 0)
BY_DVE = 5
BY_ACT = (5, 6)

GB0, GC0, HH0, Q0, K0, V0 = 0, 2, 4, 6, 12, 18


def reach(d):
    return sum(1 for w, s in PATTERNS if 0 <= d <= w and d % s == 0)


def bucket(d):
    half = 16
    if d < half:
        return d
    f = np.log(np.float32(d) / np.float32(half)) / np.float32(math.log(2048 / half)) * np.float32(half)
    return min(half + int(f), 31)


def sample_positions():
    pos = [p for p in range(PAST) if reach(PAST - p)]
    return pos


def constants():
    parts = {}
    parts["ident"] = np.eye(P)
    parts["before"] = np.triu(np.ones((P, P)), 1)
    parts["iota"] = np.tile(np.arange(1, SLOTS + 1), (P, 2))
    own = np.zeros((P, NS * H))
    for b in range(NS):
        own[b, b * H:(b + 1) * H] = 1
    parts["own"] = own
    def column(d):
        c = np.zeros(P)
        c[bucket(max(d, 0))] = 1
        c[32] = math.log(reach(d)) if reach(d) else NEG
        return c
    parts["oh"] = np.stack([column(255 - m) for m in range(384)]
                           + [column(PAST - p) for p in sample_positions()] + [column(0)], 1)
    parts["ones"] = np.ones((P, P))
    parts["limit"] = np.tile(np.arange(1, 5) * SLOTS, (P, 1))
    at, off = {}, 0
    for k, v in parts.items():
        at[k] = (off, v.shape[1])
        off += v.shape[1]
    return np.concatenate(list(parts.values()), 1).astype(np.float32), at


CONST, CONST_AT = constants()
NCONST = CONST.shape[1]


def stream():
    s = [("xp", 0), ("mp", 0)] + [("win", i) for i in range(12)]
    for i in range(4):
        s += [("qb", i), ("wk", 2 * i), ("wk", 2 * i + 1), ("wmv", i)]
    s += [("wmk", i) for i in range(4)] + [("wv", b) for b in range(NS)]
    s += [("wout", i) for i in range(4)] + [("wmq", i) for i in range(4)]
    for i in range(4):
        s += [("mqb", i), ("mk", 2 * i), ("mk", 2 * i + 1)]
    s += [("mv", b) for b in range(NS)] + [("wmo", i) for i in range(4)]
    return s


STREAM = stream()
AT = {key: n for n, key in enumerate(STREAM)}
NPRE = len(STREAM)
FILL = {1: 0, 2: 1, 4: 2, 5: 3, 7: 4, 8: 5, 10: 6, 11: 7}
PER_EXPERT = 12


def decoder_layer(nc, x_prompt, x_sample, mem_prompt, cache_win_k, cache_win_v, state_conv, cache_mem_k,
                  cache_mem_v, rel_bias_table, w_in, w_conv, w_out, ln1_g, ln1_b, w_mem_q, w_mem_k, w_mem_v,
                  w_mem_o, ln2_g, ln2_b, w_router, b_router, w_gate_up, b_gate_up, w_down, b_down, ln3_g,
                  ln3_b, const, y_prompt, y_sample, o_wk, o_wv, o_conv, o_mk, o_mv, o_sk, o_sv, o_sconv):
    ctx = ExitStack()
    with ctx:
        def sem(name):
            return ctx.enter_context(nc.semaphore(name))

        ring = ctx.enter_context(nc.sbuf_tensor("ring", [P, RING, 2048], F32))
        ARENA = 28600
        arena = ctx.enter_context(nc.sbuf_tensor("arena", [P, ARENA], F32))
        nswi = ctx.enter_context(nc.sbuf_tensor("nswi", [1, 2], I32))
        ps = ctx.enter_context(nc.psum_tensor("ps", [P, 8, 512], F32))
        psf = ps[:, :, :].rearrange("p b n -> p (b n)")
        scratch_bias = nc.dram_tensor("scratch_bias", [H, P, 384], F32, kind="Internal").ap()
        scratch_q = nc.dram_tensor("scratch_q", [NS, AW], F32, kind="Internal").ap()
        scratch_mq = nc.dram_tensor("scratch_mq", [NS, D], F32, kind="Internal").ap()
        scratch_self = nc.dram_tensor("scratch_self", [NS, H], F32, kind="Internal").ap()

        top = [0]

        def region(n):
            a = top[0]
            top[0] += n
            assert top[0] <= ARENA, top[0]
            return a

        def view(a, *dims):
            n = int(np.prod(dims))
            v = arena[:, a:a + n]
            if len(dims) == 2:
                return v.rearrange("p (a b) -> p a b", a=dims[0])
            if len(dims) == 3:
                return v.rearrange("p (a b c) -> p a b c", a=dims[0], b=dims[1])
            return v

        a_const = region(NCONST)
        cst = view(a_const, NCONST)

        def con(name):
            a, n = CONST_AT[name]
            return cst[:, a:a + n]
        ident = con("ident")
        a_small = region(700)
        small = view(a_small, 700)
        cut = [0]

        def tiny(n):
            a = cut[0]
            cut[0] += n
            assert cut[0] <= 700
            return small[:, a:a + n]

        a_xT = region(DC * T)
        xT = view(a_xT, DC, T)
        a_xh = region(3 * D)
        xh = view(a_xh, 3, D)
        a_bgu = region(2 * D)
        bgu = view(a_bgu, 2 * D)
        a_proj = region(24 * T)
        proj = view(a_proj, 24, T)
        mqT = view(a_proj + Q0 * T, DC, T)
        ks_nat = view(a_proj, AW)
        vs_nat = view(a_proj + AW, AW)
        knat = view(a_proj + V0 * T, 2, AW)
        a_mix = region(DC * T)
        mixT = view(a_mix, DC, T)
        a_vnat = region(2 * AW)
        vnat = view(a_vnat, 2, AW)
        a_bias = region(H * 256)
        bias = view(a_bias, H, 256)
        a_memT = region(DC * MT)
        memT = view(a_memT, DC, MT)
        memkT = view(a_memT, DC, MT)
        a_memv = region(2 * D)
        memv = view(a_memv, 2, D)
        memk_nat = view(a_xh, 2, D)
        qs_nat = view(a_xh + 2 * D, D)
        a_lg = region(2 * 512)
        lg = view(a_lg, 2, 512)
        a_pt = region(2 * 512)
        pt = view(a_pt, 2, 512)
        a_ss = region(200)
        ssc = view(a_ss, 200)
        es = view(a_bias, 264)
        pts = view(a_bias + 264, 2, 128)
        selfw = view(a_bias + 264 + 256, 128)
        avs = view(a_bias + 264 + 384, 2, D)
        stT = tiny(2 * 16).rearrange("p (c n) -> p c n", c=2)
        us = tiny(2 * NS).rearrange("p (c b) -> p c b", c=2)
        ul = tiny(2 * 2).rearrange("p (c k) -> p c k", c=2)
        wc = tiny(6).rearrange("p (k c) -> p k c", k=3)
        gcol = [tiny(DC) for _ in range(2)]
        bcol = [tiny(DC) for _ in range(2)]
        mx, nm, sm, rs = (tiny(4).rearrange("p (a b) -> p a b", a=2) for _ in range(4))
        ssm = tiny(8)
        stats = tiny(36).rearrange("p (t n) -> p t n", t=3)
        mv = tiny(6).rearrange("p (t n) -> p t n", t=3)
        rstd = tiny(6).rearrange("p (t n) -> p t n", t=3)
        tab = tiny(H)
        tab8 = tiny(NS * H)
        bsm = tiny(2 * H).rearrange("p (c h) -> p c h", c=2)
        brc = tiny(1)
        bself = tiny(1)
        sself = tiny(1)
        dself = tiny(H)
        a_low = a_small + cut[0]
        tiny(P)
        beforeb, onesb = (arena[:, a_low + 64 * i:a_low + 64 * i + 64].bitcast(BF16) for i in range(2))
        m0 = a_proj
        xTe = view(m0, DC, P)
        g2 = view(m0 + 1024, 512)
        u2 = view(m0 + 1536, 512)
        sg_ = view(m0 + 2048, 512)
        act_ = view(m0 + 2560, 512)
        actT = view(m0 + 3072, 4, P)
        yb = view(m0 + 3584, 2, 512)
        wr = view(m0 + 4608, DC, NX)
        m1 = a_mix
        Sel = view(m1, 3, 2, SLOTS)
        SelG = view(m1 + 384, 3, 2, SLOTS)
        SelT = view(m1 + 768, 2, T)
        selE = view(m1 + 768 + 2 * T, 2, SLOTS)
        assert 768 + 2 * T + 2 * SLOTS <= DC * T
        m2 = a_vnat
        lgt, gtm, eqm, cum, msk_, posm, gat, rex = (view(m2 + 96 * i, 3, NX) for i in range(8))
        msk = arena[:, m2 + 384:m2 + 432].bitcast(BF16).rearrange("p (t e) -> p t e", t=3)
        lgTs = view(m2 + 768, T)
        top8 = view(m2 + 768 + T, 3, 8)
        left, rsum = (view(m2 + 792 + T + 3 * i, 3) for i in range(2))
        cmax, over, lim4 = view(m2 + 798 + T, 1), view(m2 + 799 + T, 1), view(m2 + 800 + T, 4)
        assert 804 + T <= 2 * AW
        g3 = view(a_bias, 2, D)
        yo = view(a_memT, 3, D)

        landed = [sem(f"landed{s}") for s in range(RING)]
        s_const = sem("s_const")
        s_par = sem("s_par")
        s_late = sem("s_late")
        s_g3 = sem("s_g3")
        s_stored = sem("s_stored")
        s_yst = sem("s_yst")
        s_kvst = sem("s_kvst")
        s_mst = sem("s_mst")
        s_zero = sem("s_zero")
        s_xT = sem("s_xT")
        s_xT_out = sem("s_xT_out")
        s_mT = sem("s_mT")
        s_mT_out = sem("s_mT_out")
        s_half = sem("s_half")
        s_dn = sem("s_dn")
        s_dn_out = sem("s_dn_out")
        s_bt = sem("s_bt")
        s_bt_out = sem("s_bt_out")
        s_bscr = sem("s_bscr")
        s_bias = sem("s_bias")
        s_nat = sem("s_nat")
        s_nat_out = sem("s_nat_out")
        s_qscr = sem("s_qscr")
        s_mq = [sem(f"s_mq{i}") for i in range(4)]
        s_kr2 = sem("s_kr2")
        s_ka = sem("s_ka")
        s_mr = sem("s_mr")
        s_alpha = sem("s_alpha")
        s_first = sem("s_first")
        s_yz = sem("s_yz")
        s_spread = sem("s_spread")
        s_conv = sem("s_conv")
        s_sc = sem("s_sc")
        s_nm = sem("s_nm")
        s_ex = sem("s_ex")
        s_pn = sem("s_pn")
        s_pt = sem("s_pt")
        s_pt_out = sem("s_pt_out")
        s_av = sem("s_av")
        s_av_out = sem("s_av_out")
        s_kq = sem("s_kq")
        s_kr = sem("s_kr")
        s_mkT = sem("s_mkT")
        s_mkT_out = sem("s_mkT_out")
        s_ss = sem("s_ss")
        s_sT = sem("s_sT")
        s_snm = sem("s_snm")
        s_sex = sem("s_sex")
        s_spn = sem("s_spn")
        s_spT = sem("s_spT")
        s_spT_out = sem("s_spT_out")
        s_sav = sem("s_sav")
        s_sav_out = sem("s_sav_out")
        s_sat = sem("s_sat")
        s_sat_out = sem("s_sat_out")
        s_selfw = sem("s_selfw")
        s_selfd = sem("s_selfd")
        s_ln = sem("s_ln")
        s_var = sem("s_var")
        s_sq = sem("s_sq")
        s_xh = sem("s_xh")
        s_lt = sem("s_lt")
        s_lt_out = sem("s_lt_out")
        s_lt_odd = sem("s_lt_odd")
        s_x2 = sem("s_x2")
        s_x2_out = sem("s_x2_out")
        s_rt = sem("s_rt")
        s_rt_out = sem("s_rt_out")
        s_gex = sem("s_gex")
        s_low = sem("s_low")
        s_nsw = sem("s_nsw")
        s_yo = sem("s_yo")
        s_g3d = sem("s_g3d")
        dve_own = sem("dve_own")
        e_sel = sem("e_sel")
        e_selg = sem("e_selg")
        e_sb = sem("e_sb")
        e_gx = sem("e_gx")
        e_gx_out = sem("e_gx_out")
        e_wu = sem("e_wu")
        e_gu = sem("e_gu")
        e_g2 = sem("e_g2")
        e_u2 = sem("e_u2")
        e_sig = sem("e_sig")
        e_mul = sem("e_mul")
        e_act = sem("e_act")
        e_at = sem("e_at")
        e_at_out = sem("e_at_out")
        e_du = sem("e_du")
        e_dn = sem("e_dn")
        e_yb = sem("e_yb")
        e_st = sem("e_st")
        e_st_out = sem("e_st_out")
        e_y = sem("e_y")
        e_y_out = sem("e_y_out")
        e_pos = sem("e_pos")

        def loads(n):
            return {"wk": 3, "wv": 3, "qb": 0, "mqb": 0}.get(STREAM[n][0], 1)

        def landed_at(n):
            return 16 * sum(loads(m) for m in range(n % RING, n + 1, RING))

        LBASE = [16 * sum(loads(m) for m in range(s, NPRE, RING)) for s in range(RING)]

        def arrived(eng, key):
            n = AT[key]
            if key[0] in ("qb", "mqb"):
                if key[0] == "qb":
                    eng.wait_ge(s_spread, 16 * (key[1] + 1))
                else:
                    eng.wait_ge(s_mq[key[1]], 16)
                return
            eng.wait_ge(landed[n % RING], landed_at(n))

        def slot(key):
            return ring[:, AT[key] % RING, :]

        def quarters(key):
            return slot(key).rearrange("p (k n) -> p k n", k=4)

        def halves(key):
            return slot(key).rearrange("p (k n) -> p k n", k=2)

        DENSE = ["win"] * 6 + ["wmv"] * 2 + ["wmk"] * 2 + ["wout"] * 2 + ["wmq"] * 2 + ["wmo"] * 2
        GROUP0 = {w: DENSE.index(w) for w in ("win", "wmv", "wmk", "wout", "wmq", "wmo")}
        TILE0 = {"win": 0, "wmv": 24, "wmk": 28, "wout": 32, "wmq": 40, "wmo": 48}

        def reader_done(eng, n):
            what, i = STREAM[n]
            if what == "xp":
                eng.wait_ge(s_xT, DC)
            elif what == "mp":
                eng.wait_ge(s_mT, DC)
            elif what in GROUP0:
                if i % 2 == 0:
                    eng.wait_ge(s_half, GROUP0[what] + i // 2 + 1)
                else:
                    per = 2 if what in ("wmv", "wmk") else 4
                    eng.wait_ge(s_dn, TILE0[what] + per * (i // 2 + 1))
            elif what == "qb":
                eng.wait_ge(s_kq, 2 * i + 2)
            elif what == "wk":
                eng.wait_ge(s_kr, i + 1)
            elif what == "mqb":
                if 2 * i < BY_DVE:
                    eng.wait_ge(s_kr2, min(2 * i + 2, BY_DVE))
                if 2 * i + 1 >= BY_DVE:
                    eng.wait_ge(s_kq, NS + 2 * i + 2 - BY_DVE)
            elif what == "mk":
                if i in BY_ACT:
                    eng.wait_ge(s_ka, BY_ACT.index(i) + 1)
                else:
                    eng.wait_ge(s_kr2, min(i, BY_DVE) + 1)
            else:
                eng.wait_ge(s_sav, i // 4 + 1 + (2 if what == "mv" else 0))

        gate_rows = w_gate_up[0]
        down_rows = w_down[0]
        pos = sample_positions()
        assert pos == list(range(0, 512, 16)) + list(range(512, 896, 4)) + list(range(896, PAST))

        block = ctx.enter_context(nc.Block())

        @block.sync
        def _(sp):
            sp.dma_start(ring[:, 0, :].rearrange("p (k n) -> p k n", k=2),
                         x_prompt[0].rearrange("(k p) n -> p k n", p=P)).then_inc(landed[0], 16)
            sp.dma_start(cst, const).then_inc(s_const, 16)
            sp.dma_start(xh[0:NS, 2, :], x_sample.rearrange("b s d -> (b s) d")).then_inc(s_const, 16)
            sp.dma_start(tab[0:NX, :], rel_bias_table).then_inc(s_const, 16)
            sp.dma_start(xh[0:2 * NS, 0, 0:CW], state_conv[0].rearrange("b k c -> (b k) c")).then_inc(s_const, 16)
            for n, (what, i) in enumerate(STREAM):
                if n == 0 or what in ("qb", "mqb"):
                    continue
                if n >= RING:
                    reader_done(sp, n - RING)
                done = landed[n % RING]
                two = ring[:, n % RING, :].rearrange("p (k n) -> p k n", k=2)
                if what == "mp":
                    sp.dma_start(two, mem_prompt[0].rearrange("(k p) n -> p k n", p=P)).then_inc(done, 16)
                elif what in GROUP0:
                    w = {"win": w_in, "wmk": w_mem_k, "wmv": w_mem_v, "wout": w_out, "wmq": w_mem_q,
                         "wmo": w_mem_o}[what][0]
                    r0, c0 = 512 * (i % 2), 512 * (i // 2)
                    sp.dma_start(ring[:, n % RING, :].rearrange("p (k n) -> p k n", k=4),
                                 w[r0:r0 + 512, c0:c0 + 512].rearrange("(k p) n -> p k n", p=P)).then_inc(done, 16)
                elif what in ("wk", "wv"):
                    c = (cache_win_k if what == "wk" else cache_win_v)[0, i].rearrange("s h e -> s (h e)")
                    sp.dma_start(two[0:32, 0, 0:AW],
                                 c[0:512].rearrange("(s r) n -> s r n", r=16)[:, 0, :]).then_inc(done, 16)
                    sp.dma_start(two[32:P, 0, 0:AW],
                                 c[512:896].rearrange("(s r) n -> s r n", r=4)[:, 0, :]).then_inc(done, 16)
                    sp.dma_start(two[:, 1, 0:AW], c[896:PAST]).then_inc(done, 16)
                else:
                    c = (cache_mem_k if what == "mk" else cache_mem_v)[0, i].rearrange("m h e -> m (h e)")
                    sp.dma_start(two, c.rearrange("(k p) n -> p k n", p=P)).then_inc(done, 16)

            def expert_load(e, i):
                s = (NPRE + i) % RING
                if i < 8:
                    src = gate_rows[bass.ds(e, 1), i * P:(i + 1) * P, :].rearrange("a p n -> (a p) n")
                    sp.dma_start(ring[:, s, :], src).then_inc(landed[s], 16)
                else:
                    src = down_rows[bass.ds(e, 1), (i - 8) * 2 * P:(i - 7) * 2 * P, :].rearrange(
                        "a (k p) n -> p (a k) n", p=P)
                    sp.dma_start(ring[:, s, :].rearrange("p (k n) -> p k n", k=2), src).then_inc(landed[s], 16)

            def expert_loads(e, turn):
                for i in range(PER_EXPERT):
                    if i < 7:
                        sp.wait_ge(e_wu, 7 * turn + (i + 1 - 7))
                    elif i == 7:
                        sp.wait_ge(e_gu, turn)
                    elif i < 11:
                        sp.wait_ge(e_du, 3 * turn + (i - 7 - 3))
                    else:
                        sp.wait_ge(e_dn, turn)
                    expert_load(e, i)

            for i in range(PER_EXPERT):
                reader_done(sp, NPRE + i - RING)
                expert_load(0, i)
            with sp.Fori(1, NX) as e:
                expert_loads(e, e)
            sp.wait_ge(s_nsw, 2)
            turns = sp.value_load(nswi[0:1, 1:2], min_val=NX, max_val=5 * NX)
            with sp.If(turns > NX):
                with sp.Fori(NX, turns) as turn:
                    expert_loads(turn % NX, turn)
            yp = y_prompt[0].rearrange("(k p) n -> p k n", p=P)
            for t in range(3):
                sp.wait_ge(s_yo, t + 1)
                if t < 2:
                    sp.dma_start(yp[:, t, :], yo[:, t, :]).then_inc(s_yst, 16)
                else:
                    sp.dma_start(y_sample.rearrange("b s d -> (b s) d"), yo[0:NS, 2, :]).then_inc(s_yst, 16)
            sp.wait_ge(s_yst, 16 * 3)
            sp.wait_ge(s_stored, 16 * 5)
            sp.wait_ge(s_kvst, 16 * 4)
            sp.wait_ge(s_mst, 16 * 2)

        @block.gpsimd
        def _(pool):
            nc.gpsimd.memset(tab[NX:NX + 1, :], 1.0).then_inc(s_zero, 1)
            pool.wait_ge(s_zero, 1)
            nc.gpsimd.memset(bgu, 0.0).then_inc(s_zero, 1)
            pool.wait_ge(s_const, 64)
            pool.wait_ge(s_zero, 2)
            nc.gpsimd.tensor_copy(tab8[0:NX + 1, :].rearrange("p (b h) -> p b h", b=NS),
                                  tab[0:NX + 1, :].unsqueeze(1).broadcast_to((NX + 1, NS, H))).then_inc(s_zero, 1)
            pool.dma_start(bgu[0:NX, :], b_gate_up[0]).then_inc(s_par, 16)
            with nc.allow_non_contiguous_dma(reason="columns of small parameters"):
                for k in range(3):
                    pool.dma_start(wc[:, k, :], w_conv[0, k].rearrange("(c p) -> p c", p=P)).then_inc(s_par, 16)
                for g, b, gc, bc in ((ln1_g, ln1_b, gcol[0], bcol[0]), (ln2_g, ln2_b, gcol[1], bcol[1])):
                    pool.dma_start(gc, g[0].rearrange("(c p) -> p c", p=P)).then_inc(s_par, 16)
                    pool.dma_start(bc, b[0].rearrange("(c p) -> p c", p=P)).then_inc(s_par, 16)
                pool.dma_start(brc[0:NX, :], b_router[0].rearrange("(e a) -> e a", a=1)).then_inc(s_par, 16)
            pool.dma_start(o_sconv[0, :, 0, :], state_conv[0, :, 1, :]).then_inc(s_stored, 16)
            pool.wait_ge(s_bt_out, 1)
            pool.dma_start(scratch_bias, lg[0:H, 0, 0:384].unsqueeze(1).broadcast_to((H, P, 384))).then_inc(s_bscr, 16)
            pool.wait_ge(s_bscr, 16)
            pool.dma_start(bias, bass.AP(scratch_bias.tensor, P - 1, [[383, P], [P * 384, H], [1, 256]])).then_inc(
                s_bias, 16)

            def spread(kind, src, width, i, done):
                n = AT[(kind, i)]
                reader_done(pool, n - RING)
                dst = ring[:, n % RING, 0:2 * width].rearrange("p (b n) -> p b n", b=2)
                pool.dma_start(dst, src[2 * i:2 * i + 2].unsqueeze(0).broadcast_to((P, 2, width))).then_inc(
                    done, 16)

            def products(kq, kk, width, b):
                arrived(pool, (kq, b // 2))
                arrived(pool, (kk, b))
                q = slot((kq, b // 2))[:, (b % 2) * width:(b % 2 + 1) * width]
                k = halves((kk, b))[:, :, 0:width]
                nc.gpsimd.tensor_tensor(k, k, q.unsqueeze(1).broadcast_to((P, 2, width)), ALU.mult).then_inc(
                    s_kq, 1)

            pool.wait_ge(s_nat_out, 1)
            pool.dma_start(scratch_q, qs_nat[0:NS, 0:AW]).then_inc(s_qscr, 16)
            pool.wait_ge(s_qscr, 16)
            for b in range(NS):
                if b % 2 == 0:
                    spread("qb", scratch_q, AW, b // 2, s_spread)
                products("qb", "wk", AW, b)
            pool.wait_ge(s_nat_out, 7)
            rows = lambda o: o[0, 0].rearrange("s h e -> s (h e)").rearrange("(k p) n -> p k n", p=P)
            flat = lambda o: o[0, :, 0].rearrange("b h e -> b (h e)")
            pool.dma_start(rows(o_wv), vnat).then_inc(s_kvst, 16)
            pool.dma_start(rows(o_wk), knat).then_inc(s_kvst, 16)
            pool.dma_start(flat(o_sk), ks_nat[0:NS, :]).then_inc(s_kvst, 16)
            pool.dma_start(flat(o_sv), vs_nat[0:NS, :]).then_inc(s_kvst, 16)
            with nc.allow_non_contiguous_dma(reason="conv rows, one element per channel"):
                for c in range(2):
                    pool.dma_start(o_conv[0, 0].rearrange("k (c p) -> p c k", p=P)[:, c, :],
                                   ul[:, c, :]).then_inc(s_stored, 16)
                    pool.dma_start(o_sconv[0, :, 1, :].rearrange("b (c p) -> p c b", p=P)[:, c, :],
                                   us[:, c, :]).then_inc(s_stored, 16)
            pool.wait_ge(s_selfd, 1)
            pool.dma_start(scratch_self, dself[0:NS, :]).then_inc(s_selfw, 16)
            pool.wait_ge(s_selfw, 16)
            with nc.allow_non_contiguous_dma(reason="one score per row"):
                pool.dma_start(sself[0:NS * H, 0:1], scratch_self.rearrange("b (h a) -> (b h) a", a=1)).then_inc(
                    s_selfw, 16)
            mrows = lambda o: o[0, 0].rearrange("m h e -> m (h e)").rearrange("(k p) n -> p k n", p=P)
            pool.wait_ge(s_dn_out, 32)
            pool.dma_start(mrows(o_mv), memv).then_inc(s_mst, 16)
            pool.dma_start(mrows(o_mk), memk_nat).then_inc(s_mst, 16)
            pool.wait_ge(s_nat_out, 8)
            pool.dma_start(scratch_mq, qs_nat[0:NS, :]).then_inc(s_qscr, 16)
            pool.wait_ge(s_qscr, 32)
            for i in (0, 2, 1, 3):
                spread("mqb", scratch_mq, D, i, s_mq[i])
            for b in range(BY_DVE, NS):
                products("mqb", "mk", D, b)
            pool.wait_ge(s_kvst, 64)
            pool.dma_start(wr, w_router[0].rearrange("(c p) e -> p c e", p=P)).then_inc(s_late, 16)
            pool.wait_ge(s_sat, 4)
            pool.dma_start(g3[:, 0, :], ln3_g.broadcast_to((P, D))).then_inc(s_g3, 16)
            pool.dma_start(g3[:, 1, :], ln3_b.broadcast_to((P, D))).then_inc(s_g3, 16)
            pool.wait_ge(s_yz, 1)
            pool.dma_start(yb[0:NX], b_down[0].rearrange("e (h n) -> e h n", h=2)).then_inc(s_first, 16)

        @block.scalar
        def _(act):
            for c in range(DC):
                act.wait_ge(s_xT, c + 1)
                nc.scalar.copy(xT[:, c, :], ps[:, c % 4, 0:T]).then_inc(s_xT_out, 1)

            def dense_out(n, dst, width, scale=1.0):
                act.wait_ge(s_dn, n + 1)
                nc.scalar.activation(dst, ps[:, n % 4, 0:width], ACT.Copy, scale=scale).then_inc(s_dn_out, 1)

            for n in range(24):
                dense_out(n, proj[:, n, :], T, 0.125 if Q0 <= n < K0 else 1.0)

            def expo(h, wide_):
                act.wait_ge(s_nm, h + 1)
                b = h % 2
                parts = ((0, 256), (256, 512)) if wide_ else ((0, 128), (128, 384))
                for c, (a, z) in enumerate(parts):
                    src = ps[:, 4 + b, a:z] if wide_ else lg[:, b, a:z]
                    nc.scalar.activation(lg[:, b, a:z], src, ACT.Exp, bias=nm[:, b, c:c + 1],
                                         accum_out=sm[:, b, c:c + 1]).then_inc(s_ex, 1)

            def pt_out(h, n):
                act.wait_ge(s_pt, h + 1)
                if h >= 2:
                    act.wait_ge(s_av, h - 1)
                nc.scalar.copy(pt[:, h % 2, 0:n], ps[:, 6, 0:n]).then_inc(s_pt_out, 1)

            def av_out(h):
                act.wait_ge(s_av, h + 1)
                r = E * (h % 2)
                nc.scalar.copy(mixT[r:r + E, 2 + h // 2, 0:NP_], ps[r:r + E, 7, 0:NP_]).then_inc(s_av_out, 1)

            for step in range(H + 2):
                if step < H:
                    expo(step, False)
                if 1 <= step <= H:
                    pt_out(step - 1, 384)
                if step >= 2:
                    av_out(step - 2)
                f = FILL.get(step)
                if f is not None and f % 2 == 1:
                    g = f // 2
                    for m in range(2):
                        n = 24 + 2 * g + m
                        dst = (memv if g < 2 else memk_nat)[:, m, 512 * (g % 2):512 * (g % 2) + 512]
                        dense_out(n, dst, 512)

            def sample_exp(k, n, own_score):
                act.wait_ge(s_snm, k + 1)
                nc.scalar.activation(es[0:n, 0:256], ps[0:n, 4, 0:256], ACT.Exp, bias=ssm[0:n, 2:3],
                                     accum_out=ssm[0:n, 3:4]).then_inc(s_sex, 1)
                if own_score:
                    nc.scalar.activation(es[0:n, 256:257], ssm[0:n, 0:1], ACT.Exp,
                                         bias=ssm[0:n, 2:3]).then_inc(s_sex, 1)

            def sample_av_out(k, width):
                for g in range(2):
                    act.wait_ge(s_sav, 2 * k + g + 1)
                    nc.scalar.copy(avs[:, g, 0:width], psf[:, 2048 + 1024 * g:2048 + 1024 * g + width]).then_inc(
                        s_sav_out, 1)

            def layer_norm(k):
                for t, (_, n) in enumerate(TCH):
                    act.wait_ge(s_var, 3 * k + t + 1)
                    nc.scalar.activation(rstd[0:n, t, 0:1], rstd[0:n, t, 0:1], ACT.Sqrt).then_inc(s_sq, 1)
                    if k < 2:
                        act.wait_ge(s_mr, 3 * k + t + 1)
                        nc.scalar.activation(xh[0:n, t, :], psf[0:n, 512 * ROWB[t]:512 * ROWB[t] + D], ACT.Identity,
                                             bias=mv[0:n, t, 1:2], scale=rstd[0:n, t, 1:2]).then_inc(s_xh, 1)
                if k == 2:
                    return
                for c in range(0, DC, 2):
                    act.wait_ge(s_lt, DC * k + c + 1)
                    nc.scalar.activation(xT[:, c, :], ps[:, c % 4, 0:T], ACT.Identity, bias=bcol[k][:, c:c + 1],
                                         scale=gcol[k][:, c:c + 1]).then_inc(s_lt_out, 1)

            def key_sum(b):
                act.wait_ge(s_kq, NS + b - BY_DVE + 1)
                for c in range(2):
                    for h in range(MH):
                        v = halves(("mk", b))[:, c, MT * h:MT * h + MT]
                        to = (c * NS + b) * MH + h
                        ins = nc.scalar.activation(v, v, ACT.Copy, accum_out=ssc[:, to:to + 1])
                ins.then_inc(s_ka, 1)

            sample_exp(0, NS * H, True)
            sample_av_out(0, AW)
            act.wait_ge(s_par, 16 * 9)
            act.wait_ge(s_mst, 32)
            layer_norm(0)
            for n in range(40, 48):
                dense_out(n, mqT[:, n - 40, :], T, 1.0 / 16)
            for h in range(H, H + MH + 2):
                if h < H + MH:
                    expo(h, True)
                if H + 1 <= h <= H + MH:
                    pt_out(h - 1, 512)
                if h >= H + 2:
                    act.wait_ge(s_av, h - 1)
                    j = h - 2 - H
                    nc.scalar.copy(mixT[:, 2 * j:2 * j + 2, 0:NP_],
                                   ps[:, 7, :].rearrange("p (c n) -> p c n", c=2)).then_inc(s_av_out, 1)
                if h == H + MH:
                    key_sum(BY_ACT[0])
            key_sum(BY_ACT[1])
            sample_exp(1, NS * MH, False)
            sample_av_out(1, D)
            layer_norm(1)
            for t, (_, n) in enumerate(TCH):
                act.wait_ge(s_x2, t + 1)
                b = (4, 6, 2)[t]
                nc.scalar.copy(xh[0:n, t, :], psf[0:n, 512 * b:512 * b + D]).then_inc(s_x2_out, 1)
            act.wait_ge(s_rt_out, 3)
            nc.scalar.activation(rex, rex, ACT.Exp).then_inc(s_gex, 1)

            act.wait_ge(s_nsw, 2)
            act.sem_inc(e_yb, 1)
            act.sem_inc(e_at_out, 1)
            pairs = act.value_load(nswi[0:1, 0:1], min_val=16, max_val=80)
            act.wait_ge(e_gx, 1)
            nc.scalar.copy(xTe, ps[:, 6:8, :].rearrange("p b (c n) -> p (b c) n", n=P)).then_inc(e_gx_out, 1)
            with act.Fori(0, pairs) as it:
                for a in range(2):
                    act.wait_ge(e_g2, 2 * it + (a + 1))
                    nc.scalar.activation(sg_, g2, ACT.Sigmoid, scale=1.702).then_inc(e_sig, 1)
                    if a == 1:
                        act.wait_ge(e_gx, it + 2)
                        nc.scalar.copy(xTe, ps[:, 6:8, :].rearrange("p b (c n) -> p (b c) n", n=P)).then_inc(
                            e_gx_out, 1)
                    act.wait_ge(e_at, 2 * it + (a + 2))
                    nc.scalar.copy(actT, ps[:, 2, :].rearrange("p (q n) -> p q n", q=4)).then_inc(e_at_out, 1)
                act.wait_ge(e_dn, 2 * it + 2)
                nc.scalar.copy(yb, ps[:, 4:6, :]).then_inc(e_yb, 1)
            layer_norm(2)

        @block.vector
        def _(dve):
            own = [0]

            def link(ins):
                own[0] += 1
                ins.then_inc(dve_own, 1)
                dve.wait_ge(dve_own, own[0])

            dve.wait_ge(s_const, 64)
            for c in range(DC):
                dve.wait_ge(s_mT, c + 1)
                nc.vector.tensor_copy(memT[:, c, :], ps[:, 4 + c % 4, 0:MT]).then_inc(s_mT_out, 1)
            nc.vector.tensor_copy(beforeb, con("before")).then_inc(s_low, 1)
            nc.vector.tensor_copy(onesb, con("ones")).then_inc(s_low, 1)
            dve.wait_ge(s_bt, 1)
            nc.vector.tensor_copy(lg[0:H, 0, 0:384], ps[0:H, 4, 0:384]).then_inc(s_bt_out, 1)
            nc.vector.tensor_copy(bsm, ps[:, 5, 0:2 * H].rearrange("p (c h) -> p c h", c=2)).then_inc(s_bt_out, 1)
            nc.vector.tensor_copy(bself[0:NS * H, :], ps[0:NS * H, 5, 32:33]).then_inc(s_bt_out, 1)
            nc.vector.tensor_copy(stT, ps[:, 6, 0:32].rearrange("p (c n) -> p c n", c=2)).then_inc(s_bt_out, 1)

            dve.wait_ge(s_dn_out, 6)
            dve.wait_ge(s_par, 16 * 9)
            dve.wait_ge(s_bt_out, 4)
            u = proj[:, GC0:GC0 + 2, :]
            link(nc.vector.tensor_tensor(u, u, proj[:, HH0:HH0 + 2, :], ALU.mult))
            nc.vector.tensor_copy(us, u[:, :, NP_:T]).then_inc(s_conv, 1)
            nc.vector.tensor_copy(ul, u[:, :, NP_ - 2:NP_]).then_inc(s_conv, 1)
            link(nc.vector.tensor_scalar(mixT[:, 0, :], u[:, 0, :], wc[:, 2, 0:1], None, ALU.mult))
            link(nc.vector.tensor_scalar(mixT[:, 1, :], u[:, 1, :], wc[:, 2, 1:2], None, ALU.mult))
            for tap, back in ((1, 1), (0, 2)):
                for c in range(2):
                    o = mixT[:, c, back:NP_]
                    link(nc.vector.scalar_tensor_tensor(o, u[:, c, 0:NP_ - back], wc[:, tap, c:c + 1], o,
                                                        ALU.mult, ALU.add))
                    o = mixT[:, c, NP_:T]
                    st = stT[:, c, :].rearrange("p (b k) -> p k b", k=2)[:, tap, :]
                    link(nc.vector.scalar_tensor_tensor(o, st, wc[:, tap, c:c + 1], o, ALU.mult, ALU.add))
            link(nc.vector.tensor_tensor(mixT[:, 0:2, :], mixT[:, 0:2, :], proj[:, GB0:GB0 + 2, :], ALU.mult))

            def rows_out(k, dst, n, width):
                b = (4, 4, 6, 4, 6, 4, 6)[k] if k < 7 else 4
                dve.wait_ge(s_nat, k + 1)
                nc.vector.tensor_copy(dst, psf[0:n, 512 * b:512 * b + width]).then_inc(s_nat_out, 1)

            rows_out(0, qs_nat[0:NS, 0:AW], NS, AW)
            rows_out(1, vnat[:, 0, :], P, AW)
            rows_out(2, vnat[:, 1, :], P, AW)
            rows_out(3, vs_nat[0:NS, :], NS, AW)
            rows_out(4, knat[:, 0, :], P, AW)
            rows_out(5, knat[:, 1, :], P, AW)
            rows_out(6, ks_nat[0:NS, :], NS, AW)
            dve.wait_ge(s_nat_out, 7)
            dve.wait_ge(s_qscr, 16)
            q_s = qs_nat[0:NS, 0:AW]
            link(nc.vector.tensor_tensor(q_s, q_s, ks_nat[0:NS, :], ALU.mult))
            nc.vector.tensor_reduce(dself[0:NS, :], q_s.rearrange("p (h e) -> p h e", h=H), AX.X, ALU.add).then_inc(
                s_selfd, 1)

            def head_max(h):
                b = h % 2
                dve.wait_ge(s_sc, h + 1)
                if h == 0:
                    dve.wait_ge(s_bias, 16)
                if h >= 2:
                    dve.wait_ge(s_pt, h - 1)
                for c, (a, z, w) in enumerate(((0, 128, 128), (128, 384, 0))):
                    nc.vector.tensor_tensor_reduce(lg[:, b, a:z], ps[:, 4 + b, a:z], bias[:, h, w:256], 1.0, -3e38,
                                                   ALU.add, ALU.max, mx[:, b, c:c + 1]).then_inc(dve_own, 1)
                    own[0] += 1
                dve.wait_ge(dve_own, own[0])
                nc.vector.tensor_scalar(nm[:, b, :], mx[:, b, :], -1.0, None, ALU.mult).then_inc(s_nm, 1)

            def head_norm(h, parts):
                b = h % 2
                dve.wait_ge(s_ex, 2 * h + 2)
                link(nc.vector.reciprocal(rs[:, b, :], sm[:, b, :]))
                for c, (a, z) in enumerate(parts):
                    ins = nc.vector.tensor_scalar(lg[:, b, a:z], lg[:, b, a:z], rs[:, b, c:c + 1], None, ALU.mult)
                    ins.then_inc(s_pn, 1)

            def key_sums(kk, width, heads, b, n_products, done):
                dve.wait_ge(s_kq, n_products)
                n = width // heads
                src = halves((kk, b))[:, :, 0:width].rearrange("p c (h e) -> p c h e", e=n)
                dst = ssc[:, 0:2 * NS * heads].rearrange("p (c b h) -> p c b h", c=2, b=NS)[:, :, b, :]
                nc.vector.tensor_reduce(dst, src, AX.X, ALU.add).then_inc(done, 1)

            def key_scores(b):
                arrived(dve, ("mqb", b // 2))
                arrived(dve, ("mk", b))
                for c in range(2):
                    for h in range(MH):
                        k = halves(("mk", b))[:, c, MT * h:MT * h + MT]
                        q = slot(("mqb", b // 2))[:, (b % 2) * D + MT * h:(b % 2) * D + MT * h + MT]
                        to = (c * NS + b) * MH + h
                        ins = nc.vector.tensor_tensor_reduce(k, k, q, 1.0, 0.0, ALU.mult, ALU.add,
                                                             ssc[:, to:to + 1])
                ins.then_inc(s_kr2, 1)

            for step in range(H + 1):
                if step < H:
                    head_max(step)
                if 2 <= step < 2 + NS:
                    key_sums("wk", AW, H, step - 2, step - 1, s_kr)
                if step < H:
                    head_norm(step, ((0, 128), (128, 384)))

            for c in range(DC):
                dve.wait_ge(s_mkT, c + 1)
                nc.vector.tensor_copy(memkT[:, c, :], ps[:, 4 + c % 4, 0:MT]).then_inc(s_mkT_out, 1)

            def sample_softmax(k, heads):
                n = NS * heads
                if k == 0:
                    dve.wait_ge(s_selfw, 32)
                    link(nc.vector.tensor_tensor(sself[0:n, :], sself[0:n, :], bself[0:n, :], ALU.add))
                dve.wait_ge(s_sT, k + 1)
                link(nc.vector.tensor_reduce(ssm[0:n, 1:2], ps[0:n, 4, 0:256], AX.X, ALU.max))
                if k == 0:
                    link(nc.vector.tensor_copy(ssm[0:n, 0:1], sself[0:n, :]))
                    link(nc.vector.tensor_tensor(ssm[0:n, 1:2], ssm[0:n, 1:2], ssm[0:n, 0:1], ALU.max))
                nc.vector.tensor_scalar(ssm[0:n, 2:3], ssm[0:n, 1:2], -1.0, None, ALU.mult).then_inc(s_snm, 1)
                dve.wait_ge(s_sex, 2 if k == 0 else 3)
                if k == 0:
                    link(nc.vector.tensor_tensor(ssm[0:n, 3:4], ssm[0:n, 3:4], es[0:n, 256:257], ALU.add))
                link(nc.vector.reciprocal(ssm[0:n, 4:5], ssm[0:n, 3:4]))
                w = 257 if k == 0 else 256
                nc.vector.tensor_scalar(es[0:n, 0:w], es[0:n, 0:w], ssm[0:n, 4:5], None, ALU.mult).then_inc(s_spn, 1)
                link(nc.vector.memset(pts, 0.0))
                if k == 0:
                    link(nc.vector.memset(selfw, 0.0))
                dve.wait_ge(s_spT, k + 1)
                if k == 0:
                    nc.vector.tensor_tensor(selfw[0:NS, 0:n], ps[0:NS, 6, 0:n], con("own")[0:NS, :],
                                            ALU.mult).then_inc(s_spT_out, 1)
                nc.vector.tensor_copy(pts[:, :, 0:n], ps[:, 5, 0:2 * n].rearrange("p (c n) -> p c n", c=2)).then_inc(
                    s_spT_out, 1)

            def sample_pick(k):
                for g in range(2):
                    dve.wait_ge(s_sat, 2 * k + g + 1)
                    base = 2048 + 1024 * g
                    c0 = NP_ + 4 * g
                    for c in range(HP if k == 0 else DC):
                        lanes = psf[:, base + P * c:base + P * c + P].rearrange("p (l h) -> p h l", l=4)
                        if k == 0:
                            for i in range(2):
                                r = E * i
                                nc.vector.tensor_copy(mixT[r:r + E, 2 + c, c0:c0 + 4],
                                                      lanes[r:r + E, 2 * c + i, :]).then_inc(s_sat_out, 1)
                        else:
                            nc.vector.tensor_copy(mixT[:, c, c0:c0 + 4], lanes[:, c // 2, :]).then_inc(s_sat_out, 1)

            def residual(n0):
                for n in range(n0, n0 + DC):
                    dve.wait_ge(s_dn, n + 1)
                    x = xT[:, n - n0, :]
                    nc.vector.scalar_tensor_tensor(x, x, ALPHA, ps[:, n % 4, 0:T], ALU.mult, ALU.add).then_inc(
                        s_dn_out, 1)

            def layer_norm(k):
                def rows(t):
                    return psf[0:TCH[t][1], 512 * ROWB[t]:512 * ROWB[t] + D]

                def stats_of(t):
                    n = TCH[t][1]
                    dve.wait_ge(s_ln, 3 * k + t + 1)
                    for j in range(2):
                        own[0] += 1
                        nc.vector.bn_stats(stats[0:n, t, 6 * j:6 * j + 6], ps[0:n, ROWB[t] + j, :]).then_inc(
                            dve_own, 1)
                    dve.wait_ge(dve_own, own[0])
                    link(nc.vector.bn_aggr(mv[0:n, t, :], stats[0:n, t, :]))
                    nc.vector.tensor_scalar(rstd[0:n, t, 0:1], mv[0:n, t, 1:2], EPS, None, ALU.add).then_inc(s_var, 1)

                def scale_of(t):
                    n = TCH[t][1]
                    dve.wait_ge(s_sq, 3 * k + t + 1)
                    link(nc.vector.reciprocal(rstd[0:n, t, 1:2], rstd[0:n, t, 0:1]))
                    if k < 2:
                        nc.vector.scalar_tensor_tensor(mv[0:n, t, 1:2], mv[0:n, t, 0:1], -1.0, rstd[0:n, t, 1:2],
                                                       ALU.mult, ALU.mult).then_inc(s_mr, 1)

                def centred(t):
                    n = TCH[t][1]
                    nc.vector.scalar_tensor_tensor(yo[0:n, t, :], rows(t), mv[0:n, t, 0:1], g3[0:n, 0, :],
                                                   ALU.subtract, ALU.mult).then_inc(s_g3d, 1)

                def finished(t):
                    n = TCH[t][1]
                    dve.wait_ge(s_g3d, t + 1)
                    nc.vector.scalar_tensor_tensor(yo[0:n, t, :], yo[0:n, t, :], rstd[0:n, t, 1:2], g3[0:n, 1, :],
                                                   ALU.mult, ALU.add).then_inc(s_yo, 1)

                if k == 2:
                    dve.wait_ge(s_g3, 32)
                    for t in range(3):
                        stats_of(t)
                        centred(t)
                        scale_of(t)
                        finished(t)
                    return
                stats_of(0)
                stats_of(1)
                scale_of(0)
                stats_of(2)
                scale_of(1)
                scale_of(2)
                for c in range(1, DC, 2):
                    dve.wait_ge(s_lt, DC * k + c + 1)
                    nc.vector.tensor_scalar(xT[:, c, :], ps[:, c % 4, 0:T], gcol[k][:, c:c + 1],
                                            bcol[k][:, c:c + 1], ALU.mult, ALU.add).then_inc(s_lt_odd, 1)

            dve.wait_ge(s_kr, NS)
            sc4 = ssc[:, 0:2 * NS * H].rearrange("p (c b h) -> p c b h", c=2, b=NS)
            for c in range(2):
                nc.vector.tensor_tensor(sc4[:, c], sc4[:, c], bsm[:, c, :].unsqueeze(1).broadcast_to((P, NS, H)),
                                        ALU.add).then_inc(s_ss, 1)
            sample_softmax(0, H)
            sample_pick(0)
            residual(32)
            layer_norm(0)

            rows_out(7, qs_nat[0:NS, :], NS, D)
            def mem_head_max(h):
                b = h % 2
                dve.wait_ge(s_sc, h + 1)
                link(nc.vector.tensor_reduce(mx[:, b, :], ps[:, 4 + b, :].rearrange("p (c m) -> p c m", c=2), AX.X,
                                             ALU.max))
                dve.wait_ge(s_pt, h - 1)
                nc.vector.tensor_scalar(nm[:, b, :], mx[:, b, :], -1.0, None, ALU.mult).then_inc(s_nm, 1)

            mem_parts = ((0, 256), (256, 512))
            mem_head_max(H)
            for h in range(H, H + MH):
                if h > H:
                    key_scores(h - 1 - H)
                head_norm(h, mem_parts)
                if h + 1 < H + MH:
                    mem_head_max(h + 1)
            for b in range(MH - 1, BY_DVE):
                key_scores(b)
            for b in range(BY_DVE, NS):
                if b not in BY_ACT:
                    key_sums("mk", D, MH, b, NS + b - BY_DVE + 1, s_kr2)
            sample_softmax(1, MH)
            sample_pick(1)
            residual(48)
            layer_norm(1)

            dve.wait_ge(s_kvst, 64)
            for tl in (lgt, posm, gat, SelT, yb):
                ins = nc.vector.memset(tl, 0.0)
                if tl is not yb:
                    own[0] += 1
                    ins.then_inc(dve_own, 1)
            ins.then_inc(s_yz, 1)
            dve.wait_ge(dve_own, own[0])
            dve.wait_ge(s_rt, 1)
            nc.vector.tensor_scalar(lgTs[0:NX, :], ps[0:NX, 0, 0:T], brc[0:NX, :], None, ALU.add).then_inc(
                s_rt_out, 1)
            dve.wait_ge(s_rt, 2)
            own[0] += 2
            nc.vector.tensor_copy(lgt[:, 0:2, :], ps[:, 1, 0:2 * NX].rearrange("p (t e) -> p t e", t=2)).then_inc(
                dve_own, 1)
            nc.vector.tensor_copy(lgt[0:NS, 2, :], ps[0:NS, 1, 2 * NX:3 * NX]).then_inc(dve_own, 1)
            dve.wait_ge(dve_own, own[0])
            for t in range(3):
                own[0] += 1
                nc.vector.max(top8[:, t, :], lgt[:, t, :]).then_inc(dve_own, 1)
            dve.wait_ge(dve_own, own[0])
            wide = lambda v: v.broadcast_to((P, 3, NX))
            own[0] += 2
            nc.vector.tensor_tensor(gtm, lgt, wide(top8[:, :, 3:4]), ALU.is_gt).then_inc(dve_own, 1)
            nc.vector.tensor_tensor(eqm, lgt, wide(top8[:, :, 3:4]), ALU.is_equal).then_inc(dve_own, 1)
            dve.wait_ge(dve_own, own[0])
            link(nc.vector.tensor_reduce(left, gtm, AX.X, ALU.add))
            for t in range(3):
                own[0] += 1
                nc.vector.tensor_tensor_scan(cum[:, t, :], con("ones")[:, 0:NX], eqm[:, t, :], left[:, t:t + 1],
                                             ALU.mult, ALU.add).then_inc(dve_own, 1)
            dve.wait_ge(dve_own, own[0])
            link(nc.vector.scalar_tensor_tensor(cum, cum, float(TOPK), eqm, ALU.is_le, ALU.mult))
            nc.vector.tensor_tensor(msk, cum, gtm, ALU.add).then_inc(s_rt_out, 1)
            nc.vector.tensor_tensor(rex, lgt, wide(top8[:, :, 0:1]), ALU.subtract).then_inc(s_rt_out, 1)
            dve.wait_ge(s_rt_out, 2)
            dve.wait_ge(s_rt, 3)
            own[0] += 2
            nc.vector.scalar_tensor_tensor(posm[:, 0:2, :], ps[:, 1, 128:192].rearrange("p (t e) -> p t e", t=2),
                                           1.0, msk[:, 0:2, :], ALU.add, ALU.mult).then_inc(dve_own, 1)
            nc.vector.scalar_tensor_tensor(posm[0:NS, 2:3, :], ps[0:NS, 1, 192:224].unsqueeze(1), 1.0,
                                           msk[0:NS, 2:3, :], ALU.add, ALU.mult).then_inc(dve_own, 1)
            dve.wait_ge(dve_own, own[0])

            four = (P, 3, 2, SLOTS)
            iota4 = con("iota").rearrange("p (a s) -> p a s", a=2).unsqueeze(1).broadcast_to(four)

            def select(q):
                nc.vector.tensor_tensor(Sel, iota4, posm[:, :, bass.ds(q, 2)].unsqueeze(3).broadcast_to(four),
                                        ALU.is_equal).then_inc(e_sel, 1)

            def pick_biases(q):
                nc.vector.tensor_copy(selE, ident[:, bass.ds(q, 2)].unsqueeze(2).broadcast_to((P, 2, SLOTS))
                                      ).then_inc(e_sb, 1)

            def advance(q, n):
                dve.wait_ge(e_sel, n)
                nc.vector.tensor_tensor(SelG, Sel, gat[:, :, bass.ds(q, 2)].unsqueeze(3).broadcast_to(four),
                                        ALU.mult).then_inc(e_selg, 1)
                nc.vector.tensor_scalar(posm[:, :, bass.ds(q, 2)], posm[:, :, bass.ds(q, 2)], -float(SLOTS), None,
                                        ALU.add).then_inc(e_pos, 1)

            select(0)
            link(nc.vector.tensor_reduce(cmax[0:1, :], ps[0:1, 1, 224:256], AX.X, ALU.max))
            link(nc.vector.tensor_scalar(lim4[0:1, :], con("limit")[0:1, :], cmax[0:1, :], None, ALU.is_lt))
            link(nc.vector.tensor_reduce(over[0:1, :], lim4[0:1, :], AX.X, ALU.add))
            nc.vector.tensor_scalar(nswi[0:1, 0:1], over[0:1, :], 16.0, 16.0, ALU.mult, ALU.add).then_inc(s_nsw, 1)
            nc.vector.tensor_scalar(nswi[0:1, 1:2], over[0:1, :], 32.0, 32.0, ALU.mult, ALU.add).then_inc(s_nsw, 1)
            pick_biases(0)
            dve.wait_ge(s_gex, 1)
            link(nc.vector.tensor_tensor(rex, rex, msk, ALU.mult))
            link(nc.vector.tensor_reduce(rsum, rex, AX.X, ALU.add))
            link(nc.vector.reciprocal(rsum, rsum))
            nc.vector.tensor_tensor(gat, rex, wide(rsum.unsqueeze(2)), ALU.mult).then_inc(s_rt_out, 1)
            dve.wait_ge(s_rt_out, 4)
            advance(0, 1)
            dve.wait_ge(s_x2, 3)
            nc.vector.tensor_scalar(xT, xT, ALPHA, None, ALU.mult).then_inc(s_alpha, 1)
            dve.wait_ge(s_rt, 4)
            for half in range(2):
                nc.vector.tensor_copy(SelT[0:NX, half, :], ps[0:NX, 3, 0:T]).then_inc(s_rt_out, 1)

            def clamp(k):
                dve.wait_ge(e_gu, k + 1)
                nc.vector.tensor_scalar(g2, ps[:, 0, :], 7.0, None, ALU.min).then_inc(e_g2, 1)
                dve.wait_ge(e_act, k + 1)
                nc.vector.tensor_scalar(u2, ps[:, 1, :], 7.0, -7.0, ALU.min, ALU.max).then_inc(e_u2, 1)

            def swiglu(k):
                dve.wait_ge(e_u2, k + 2)
                nc.vector.scalar_tensor_tensor(u2, u2, 1.0, g2, ALU.add, ALU.mult).then_inc(e_mul, 1)
                dve.wait_ge(e_mul, k + 1)
                dve.wait_ge(e_sig, k + 1)
                dve.wait_ge(e_at, k + 1)
                nc.vector.tensor_tensor(act_, u2, sg_, ALU.mult).then_inc(e_act, 1)

            def add_scattered(n):
                dve.wait_ge(e_y_out, DC * n + 1)
                for c in range(DC):
                    dve.wait_ge(e_y, DC * n + (c + 1))
                    nc.vector.tensor_tensor(xT[:, c, :], xT[:, c, :], ps[:, 2 + c % 2, 0:T], ALU.add).then_inc(
                        e_y_out, 1)

            dve.wait_ge(s_alpha, 1)
            for first in (e_u2, e_st_out, e_act, e_y_out):
                dve.sem_inc(first, 1)
            pairs = dve.value_load(nswi[0:1, 0:1], min_val=16, max_val=80)
            with dve.Fori(0, pairs) as it:
                clamp(2 * it)
                swiglu(2 * it)
                add_scattered(it)
                dve.wait_ge(e_st, it + 1)
                nc.vector.tensor_copy(SelT[:, 0, :], ps[:, 3, 0:T]).then_inc(e_st_out, 1)
                nc.vector.tensor_copy(SelT[0:64, 1, :], ps[64:P, 3, 0:T]).then_inc(e_st_out, 1)
                nc.vector.tensor_copy(SelT[64:P, 1, :], ps[0:64, 3, 0:T]).then_inc(e_st_out, 1)
                q = ((it + 1) % 16) * 2
                dve.wait_ge(e_pos, it + 1)
                dve.wait_ge(e_selg, it + 1)
                select(q)
                advance(q, it + 2)
                clamp(2 * it + 1)
                pick_biases(q)
                swiglu(2 * it + 1)
            add_scattered(pairs)
            dve.wait_ge(s_mst, 32)
            dve.wait_ge(e_y_out, DC * pairs + (DC + 1))
            layer_norm(2)

        @block.tensor
        def _(pe):
            mm = nc.tensor.matmul
            tp = nc.tensor.transpose
            pe.wait_ge(s_const, 64)
            pe.wait_ge(s_zero, 3)
            arrived(pe, ("xp", 0))
            x2 = halves(("xp", 0))
            for c in range(DC):
                if c >= 4:
                    pe.wait_ge(s_xT_out, c - 3)
                cols = slice(P * c, P * c + P)
                tp(ps[:, c % 4, 0:P], x2[:, 0, cols], ident)
                tp(ps[:, c % 4, P:2 * P], x2[:, 1, cols], ident)
                tp(ps[:, c % 4, NP_:T], xh[0:NS, 2, cols], ident[0:NS, 0:NS]).then_inc(s_xT, 1)
            arrived(pe, ("mp", 0))
            m2_ = halves(("mp", 0))
            for c in range(DC):
                if c >= 4:
                    pe.wait_ge(s_mT_out, c - 3)
                tp(ps[:, 4 + c % 4, 0:P], m2_[:, 0, P * c:P * c + P], ident)
                tp(ps[:, 4 + c % 4, P:2 * P], m2_[:, 1, P * c:P * c + P], ident).then_inc(s_mT, 1)
            pe.wait_ge(s_mT_out, DC)
            oh = con("oh")[0:NX + 1, :]
            tb = tab[0:NX + 1, :]
            mm(ps[0:H, 4, 0:384], tb, oh[:, 0:384], start=True, stop=True)
            for c in range(2):
                mm(ps[:, 5, c * H:(c + 1) * H], oh[:, 384 + c * P:384 + (c + 1) * P], tb, start=True, stop=True)
            mm(ps[0:NS * H, 5, 32:33], tab8[0:NX + 1, :], oh[:, 640:641], start=True, stop=True)
            for c in range(2):
                ins = tp(ps[:, 6, 16 * c:16 * c + 16], xh[0:2 * NS, 0, P * c:P * c + P], ident[0:2 * NS, 0:2 * NS])
            ins.then_inc(s_bt, 1)

            def dense_half(what, i, tiles):
                arrived(pe, (what, i))
                w = quarters((what, i))
                count = len(tiles)
                n0 = TILE0[what] + count * (i // 2)
                for j in range(count):
                    n = n0 + j
                    if i % 2 == 0 and n >= 4:
                        pe.wait_ge(s_dn_out, n - 3)
                    out, lhs, rhs = tiles[j]
                    for k in range(4):
                        kk = 4 * (i % 2) + k
                        ins = mm(out(n), lhs(w, k, kk), rhs(w, k, kk), start=(kk == 0), stop=(kk == 7))
                    if i % 2:
                        ins.then_inc(s_dn, 1)
                if i % 2 == 0:
                    ins.then_inc(s_half, 1)

            def columns(x):
                return [(lambda n: ps[:, n % 4, 0:T],
                         lambda w, k, kk, j=j: w[:, k, P * j:P * j + P],
                         lambda w, k, kk: x[:, kk, :]) for j in range(4)]

            def token_rows(x):
                return [(lambda n: ps[:, n % 4, :],
                         lambda w, k, kk, m=m: x[:, kk, P * m:P * m + P],
                         lambda w, k, kk: w[:, k, :]) for m in range(2)]

            pe.wait_ge(s_xT_out, DC)
            for i in range(6):
                dense_half("win", i, columns(xT))

            def turn(k, src, col, n, chunks):
                b = (4, 4, 6, 4, 6, 4, 6)[k] if k < 7 else 4
                if k in (3, 4, 5, 6):
                    pe.wait_ge(s_nat_out, k - 1)
                for c in range(chunks):
                    ins = tp(psf[0:n, 512 * b + P * c:512 * b + P * c + P], src[:, c, col:col + n], ident)
                ins.then_inc(s_nat, 1)

            pe.wait_ge(s_dn_out, 12)
            pe.wait_ge(s_bt_out, 4)
            turn(0, proj[:, Q0:K0, :], NP_, NS, HP)
            for i in range(6, 12):
                dense_half("win", i, columns(xT))
            pe.wait_ge(s_dn_out, 24)
            pe.wait_ge(s_nat_out, 1)
            for k, (src, t) in enumerate([(V0, 0), (V0, 1), (V0, 2), (K0, 0), (K0, 1), (K0, 2)]):
                turn(k + 1, proj[:, src:src + HP, :], TCH[t][0], TCH[t][1], HP)

            def scores(h):
                r, c, b = E * (h % 2), h // 2, 4 + h % 2
                if h >= 2:
                    pe.wait_ge(s_nm, h - 1)
                q = proj[r:r + E, Q0 + c, :]
                k = proj[r:r + E, K0 + c, :]
                mm(ps[:, b, 0:P], q[:, 0:P], k[:, 0:P], start=True, stop=True)
                mm(ps[:, b, P:3 * P], q[:, P:2 * P], k[:, 0:2 * P], start=True, stop=True).then_inc(s_sc, 1)

            def probs_turned(h):
                pe.wait_ge(s_pn, 2 * h + 2)
                if h >= 1:
                    pe.wait_ge(s_pt_out, h)
                for j in range(3):
                    ins = tp(ps[:, 6, P * j:P * j + P], lg[:, h % 2, P * j:P * j + P], ident)
                ins.then_inc(s_pt, 1)

            def values(h):
                pe.wait_ge(s_pt_out, h + 1)
                if h >= 1:
                    pe.wait_ge(s_av_out, h)
                r = E * (h % 2)
                v = vnat[:, :, E * h:E * h + E]
                mm(ps[r:r + E, 7, 0:P], v[:, 0, :], pt[:, h % 2, 0:P], start=True, stop=True)
                mm(ps[r:r + E, 7, P:NP_], v[:, 0, :], pt[:, h % 2, P:NP_], start=True, stop=False)
                mm(ps[r:r + E, 7, P:NP_], v[:, 1, :], pt[:, h % 2, NP_:NP_ + P], start=False,
                   stop=True).then_inc(s_av, 1)

            pe.wait_ge(s_nat_out, 7)
            for step in range(H + 2):
                if step < H:
                    scores(step)
                if 1 <= step <= H:
                    probs_turned(step - 1)
                if step >= 2:
                    values(step - 2)
                f = FILL.get(step)
                if f is not None:
                    dense_half("wmv" if f < 4 else "wmk", f % 4, token_rows(memT))
            pe.wait_ge(s_dn_out, 32)
            for c in range(DC):
                if c == 0:
                    pe.wait_ge(s_av_out, H)
                if c >= 4:
                    pe.wait_ge(s_mkT_out, c - 3)
                for m in range(2):
                    ins = tp(ps[:, 4 + c % 4, P * m:P * m + P], memk_nat[:, m, P * c:P * c + P], ident)
                ins.then_inc(s_mkT, 1)

            def sample_attention(k, heads, vv, width):
                n = NS * heads
                if k == 0:
                    pe.wait_ge(s_mkT_out, DC)
                    pe.wait_ge(s_ss, 2)
                else:
                    pe.wait_ge(s_av_out, H + MH)
                    pe.wait_ge(s_kr2, NS - len(BY_ACT))
                    pe.wait_ge(s_ka, len(BY_ACT))
                for c in range(2):
                    ins = tp(ps[0:n, 4, P * c:P * c + P], ssc[:, n * c:n * c + n], ident)
                ins.then_inc(s_sT, 1)
                pe.wait_ge(s_spn, k + 1)
                for c in range(2):
                    ins = tp(ps[:, 5, n * c:n * c + n], es[0:n, P * c:P * c + P], ident[0:n, 0:n])
                if k == 0:
                    ins = mm(ps[0:NS, 6, 0:n], es[0:n, 256:257].broadcast_to((n, NS)), ident[0:n, 0:n],
                             start=True, stop=True)
                ins.then_inc(s_spT, 1)
                pe.wait_ge(s_spT_out, 2 if k == 0 else 3)
                for g in range(2):
                    terms = [0, 1, 2] if k == 0 else [0, 1]
                    for a in range(0, width, 512):
                        z = min(a + 512, width)
                        for t in terms:
                            for lane in range(4):
                                b = 4 * g + lane
                                if a == 0 and t == 0:
                                    arrived(pe, (vv, b))
                                out = psf[32 * lane:32 * lane + 32, 2048 + 1024 * g + a:2048 + 1024 * g + z]
                                if t < 2:
                                    w = pts[:, t, heads * b:heads * b + 32]
                                    v = halves((vv, b))[:, t, a:z]
                                else:
                                    w = selfw[0:NS, heads * b:heads * b + 32]
                                    v = vs_nat[0:NS, a:z]
                                ins = mm(out, w, v, start=(t == 0), stop=(t == terms[-1]))
                    ins.then_inc(s_sav, 1)
                for g in range(2):
                    pe.wait_ge(s_sav_out, 2 * k + g + 1)
                    for c in range(width // P):
                        a = 2048 + 1024 * g + P * c
                        ins = tp(psf[:, a:a + P], avs[:, g, P * c:P * c + P], ident)
                    ins.then_inc(s_sat, 1)

            sample_attention(0, H, "wv", AW)
            pe.wait_ge(s_sat_out, 2 * H)
            for i in range(4):
                dense_half("wout", i, columns(mixT))

            def layer_norm(k):
                if k < 2:
                    pe.wait_ge(s_dn_out, 40 if k == 0 else 56)
                for t, (t0, n) in enumerate(TCH):
                    b = ROWB[t]
                    for c in range(DC):
                        ins = tp(psf[0:n, 512 * b + P * c:512 * b + P * c + P], xT[:, c, t0:t0 + n], ident)
                    ins.then_inc(s_ln, 1)
                if k == 2:
                    return
                pe.wait_ge(s_xh, 3 * k + 3)
                for c in range(DC):
                    if c >= 4:
                        pe.wait_ge(s_lt_odd if c % 2 else s_lt_out, 4 * k + (c - 4) // 2 + 1)
                    for t, (t0, n) in enumerate(TCH):
                        ins = tp(ps[:, c % 4, t0:t0 + n], xh[0:n, t, P * c:P * c + P], ident[0:n, 0:n])
                    ins.then_inc(s_lt, 1)
                pe.wait_ge(s_lt_out, 4 * k + 4)
                pe.wait_ge(s_lt_odd, 4 * k + 4)

            layer_norm(0)
            for i in range(4):
                dense_half("wmq", i, columns(xT))
            pe.wait_ge(s_dn_out, 48)
            turn(7, mqT, NP_, NS, DC)
            for h in range(H, H + MH + 2):
                j = h - H
                if j < MH:
                    if j >= 2:
                        pe.wait_ge(s_ex, 2 * h - 2)
                    if j == 0:
                        pe.wait_ge(s_nat_out, 8)
                    for qc in range(2):
                        for ec in range(2):
                            ins = mm(ps[:, 4 + h % 2, MT * qc:MT * qc + MT], mqT[:, 2 * j + ec, P * qc:P * qc + P],
                                     memkT[:, 2 * j + ec, :], start=(ec == 0), stop=(ec == 1))
                    ins.then_inc(s_sc, 1)
                if 1 <= j <= MH:
                    pe.wait_ge(s_pn, 2 * h)
                    pe.wait_ge(s_pt_out, h - 1)
                    for qc in range(2):
                        for mc in range(2):
                            ins = tp(ps[:, 6, MT * mc + P * qc:MT * mc + P * qc + P],
                                     lg[:, (h - 1) % 2, MT * qc + P * mc:MT * qc + P * mc + P], ident)
                    ins.then_inc(s_pt, 1)
                if j >= 2:
                    pe.wait_ge(s_pt_out, h - 1)
                    pe.wait_ge(s_av_out, h - 2)
                    for ec in range(2):
                        c0 = MT * (j - 2) + P * ec
                        for mc in range(2):
                            ins = mm(ps[:, 7, NP_ * ec:NP_ * ec + NP_], memv[:, mc, c0:c0 + P],
                                     pt[:, h % 2, MT * mc:MT * mc + MT], start=(mc == 0), stop=(mc == 1))
                    ins.then_inc(s_av, 1)
            sample_attention(1, MH, "mv", D)
            pe.wait_ge(s_sat_out, 2 * H + 2 * DC)
            for i in range(4):
                dense_half("wmo", i, columns(mixT))
            layer_norm(1)

            pe.wait_ge(s_late, 16)
            for c in range(DC):
                ins = mm(ps[0:NX, 0, 0:T], wr[:, c, :], xT[:, c, :], start=(c == 0), stop=(c == 7))
            ins.then_inc(s_rt, 1)

            def x2_rows(t):
                (t0, n), b = TCH[t], (4, 6, 2)[t]
                for c in range(DC):
                    ins = tp(psf[0:n, 512 * b + P * c:512 * b + P * c + P], xT[:, c, t0:t0 + n], ident)
                ins.then_inc(s_x2, 1)

            x2_rows(0)
            pe.wait_ge(s_rt_out, 1)
            for t, (t0, n) in enumerate(TCH):
                ins = tp(ps[0:n, 1, NX * t:NX * t + NX], lgTs[0:NX, t0:t0 + n], ident[0:NX, 0:NX])
            ins.then_inc(s_rt, 1)
            x2_rows(1)
            x2_rows(2)
            pe.wait_ge(s_rt_out, 2)
            pe.wait_ge(s_low, 2)
            for t, (t0, n) in enumerate(TCH):
                for c in range(t + 1):
                    m = TCH[c][1]
                    w = (beforeb if c == t else onesb)[0:m, 0:n]
                    mm(ps[0:n, 1, 128 + NX * t:128 + NX * t + NX], w, msk[0:m, c, :], start=(c == 0), stop=(c == t))
            for c in range(3):
                m = TCH[c][1]
                ins = mm(ps[0:1, 1, 224:256], onesb[0:m, 0:1], msk[0:m, c, :], start=(c == 0), stop=(c == 2))
            ins.then_inc(s_rt, 1)

            def gather():
                for c in range(DC):
                    for t, (_, n) in enumerate(TCH):
                        ins = mm(ps[:, 6 + c // 4, P * (c % 4):P * (c % 4) + P], xh[0:n, t, P * c:P * c + P],
                                 Sel[0:n, t].rearrange("p a s -> p (a s)"), start=(t == 0), stop=(t == 2))
                ins.then_inc(e_gx, 1)

            pe.wait_ge(s_x2_out, 3)
            pe.wait_ge(e_sel, 1)
            gather()
            pe.wait_ge(s_rt_out, 4)
            for t, (t0, n) in enumerate(TCH):
                ins = tp(ps[0:NX, 3, t0:t0 + n], gat[0:n, t, :], ident[0:n, 0:n])
            ins.then_inc(s_rt, 1)
            pe.wait_ge(s_nsw, 2)

            def eslot(i):
                return ring[:, (NPRE + i) % RING, :]

            def gate_up(it, a):
                first = True
                for c in range(-1, 8):
                    if c >= 0:
                        s = (NPRE + c) % RING
                        pe.wait_ge(landed[s], 32 * it + (16 * a + 16 + LBASE[s]))
                        w, x = eslot(c), xTe[:, c, SLOTS * a:SLOTS * a + SLOTS]
                    else:
                        w, x = bgu, selE[:, a, :]
                    for gu in range(2):
                        for j in range(2):
                            ins = mm(ps[64 * j:64 * j + 64, gu, :], x,
                                     w[:, D * gu + 512 * j:D * gu + 512 * j + 512], start=(c < 0), stop=(c == 7),
                                     skip_group_check=True)
                    if 0 <= c < 7:
                        ins.then_inc(e_wu, 1)
                ins.then_inc(e_gu, 1)

            def turn_act(it, a):
                for q in range(4):
                    ins = tp(ps[:, 2, P * q:P * q + P], act_[:, P * q:P * q + P], ident)
                ins.then_inc(e_at, 1)

            def down(it, a):
                for i in range(4):
                    s = (NPRE + 8 + i) % RING
                    pe.wait_ge(landed[s], 32 * it + (16 * a + 16 + LBASE[s]))
                    w = eslot(8 + i).rearrange("p (k n) -> p k n", k=2)
                    for kk in range(2):
                        m = 2 * i + kk
                        x = actT[:, m % 4, 64 * (m // 4):64 * (m // 4) + 64]
                        for j in range(2):
                            half = j if a == 0 else 1 - j
                            ins = mm(ps[64 * j:64 * j + 64, 4 + half, :], x, w[:, kk, 512 * half:512 * half + 512],
                                     start=(m == 0), stop=(m == 7), skip_group_check=True)
                    ins.then_inc(e_du if i < 3 else e_dn, 1)

            def scatter():
                for c in range(DC):
                    half = c // 4
                    if c >= 2:
                        pe.wait_ge(e_y_out, scattered[0] + c)
                    mm(ps[:, 2 + c % 2, 0:T], yb[:, half, P * (c % 4):P * (c % 4) + P], SelT[:, half, :],
                       start=True, stop=True).then_inc(e_y, 1)

            scattered = [0]
            pe.sem_inc(e_at, 1)
            pairs = pe.value_load(nswi[0:1, 0:1], min_val=16, max_val=80)
            pe.wait_ge(s_par, 16 * 9)
            with pe.Fori(0, pairs) as it:
                scattered[0] = DC * it
                pe.wait_ge(e_gx_out, it + 1)
                pe.wait_ge(e_sb, it + 1)
                pe.wait_ge(e_u2, 2 * it + 1)
                gate_up(it, 0)
                pe.wait_ge(s_first, 16)
                pe.wait_ge(s_rt_out, 6)
                pe.wait_ge(s_alpha, 1)
                pe.wait_ge(e_yb, it + 1)
                pe.wait_ge(e_st_out, 3 * it + 1)
                pe.wait_ge(e_at_out, 2 * it + 1)
                scatter()
                pe.wait_ge(e_y_out, DC * it + (DC + 1))
                pe.wait_ge(e_selg, it + 1)
                for t, (t0, n) in enumerate(TCH):
                    ins = tp(ps[:, 3, t0:t0 + n], SelG[0:n, t].rearrange("p a s -> p (a s)"), ident[0:n, 0:n])
                ins.then_inc(e_st, 1)
                pe.wait_ge(e_act, 2 * it + 2)
                turn_act(it, 0)
                pe.wait_ge(e_at_out, 2 * it + 2)
                down(it, 0)
                pe.wait_ge(e_u2, 2 * it + 2)
                gate_up(it, 1)
                pe.wait_ge(e_sel, it + 2)
                gather()
                pe.wait_ge(e_act, 2 * it + 3)
                turn_act(it, 1)
                pe.wait_ge(e_at_out, 2 * it + 3)
                down(it, 1)
            scattered[0] = DC * pairs
            pe.wait_ge(e_yb, pairs + 1)
            pe.wait_ge(e_st_out, 3 * pairs + 1)
            scatter()
            pe.wait_ge(e_y_out, DC * pairs + (DC + 1))
            layer_norm(2)


_INS = ["x_prompt", "x_sample", "mem_prompt", "cache_win_k", "cache_win_v", "state_conv", "cache_mem_k",
        "cache_mem_v", "rel_bias_table", "w_in", "w_conv", "w_out", "ln1_g", "ln1_b", "w_mem_q", "w_mem_k",
        "w_mem_v", "w_mem_o", "ln2_g", "ln2_b", "w_router", "b_router", "w_gate_up", "b_gate_up", "w_down",
        "b_down", "ln3_g", "ln3_b"]
_OUTS = [(1, NP_, D), (NS, 1, D), (1, 1, NP_, H, E), (1, 1, NP_, H, E), (1, 1, 2, CW), (1, 1, MT, MH, D // MH),
         (1, 1, MT, MH, D // MH), (1, NS, 1, H, E), (1, NS, 1, H, E), (1, NS, 2, CW)]


def kernel(**inputs):
    import numpy as _np
    import concourse.bacc as _bacc
    from concourse import mybir as _mybir
    from concourse.bass_utils import run_bass_kernel_spmd as _run

    nc = _bacc.Bacc("TRN2", target_bir_lowering=False, num_devices=1)
    arrays, args = {}, []
    for name in _INS:
        a = _np.ascontiguousarray(inputs[name])
        arrays[f"in_{name}_dram"] = a
        args.append(nc.dram_tensor(f"in_{name}_dram", a.shape, _mybir.dt.from_np(a.dtype), kind="ExternalInput").ap())
    arrays["shape_constants"] = CONST
    args.append(nc.dram_tensor("shape_constants", CONST.shape, _mybir.dt.float32, kind="ExternalInput").ap())
    for i, shape in enumerate(_OUTS):
        args.append(nc.dram_tensor(f"out_{i}_dram", shape, _mybir.dt.float32, kind="ExternalOutput").ap())
    decoder_layer(nc, *args)
    r = _run(nc, [arrays], core_ids=[0])
    return tuple(r.results[0][f"out_{i}_dram"] for i in range(len(_OUTS)))
```

```python
import math
from contextlib import ExitStack

import numpy as np

import concourse.bass as bass
from concourse import mybir

F32 = mybir.dt.float32
BF16 = mybir.dt.bfloat16
F32R = mybir.dt.float32r
I32 = mybir.dt.int32
ALU = mybir.AluOpType
ACT = mybir.ActivationFunctionType
AX = mybir.AxisListType

P = 128
D = 1024
DC = D // P
NP_ = 256
NS = 8
T = NP_ + NS
TCH = [(0, P), (P, P), (2 * P, NS)]
CW = 256
H = 12
E = 64
AW = H * E
HP = H // 2
NPROJ = 3 * CW + 3 * AW
MH = 4
MT = 256
NX = 32
TOPK = 4
SLOTS = 64
EPS = 1e-5
ALPHA = 2 ** 0.25
PAST = 1024
PATTERNS = ((128, 1), (512, 4), (2048, 16))
NEG = -1e30
RING = 12
ROWB = (4, 6, 0)
LASTB = (6, 2, 0)
LORDER = (1, 0, 2)
MEM_PAIRS = (2, 0, 3, 1)
BY_DVE = (4, 0, 1, 2, 3)
BY_POOL = (5, 6, 7)
BY_ACT = (5, 6)

GB0, GC0, HH0, Q0, K0, V0 = 0, 2, 4, 6, 12, 18


def reach(d):
    return sum(1 for w, s in PATTERNS if 0 <= d <= w and d % s == 0)


def bucket(d):
    half = 16
    if d < half:
        return d
    f = np.log(np.float32(d) / np.float32(half)) / np.float32(math.log(2048 / half)) * np.float32(half)
    return min(half + int(f), 31)


def sample_positions():
    pos = [p for p in range(PAST) if reach(PAST - p)]
    return pos


def constants():
    parts = {}
    parts["ident"] = np.eye(P)
    parts["before"] = np.triu(np.ones((P, P)), 1)
    parts["iota"] = np.tile(np.arange(1, SLOTS + 1), (P, 2))
    own = np.zeros((P, NS * H))
    for b in range(NS):
        own[b, b * H:(b + 1) * H] = 1
    parts["own"] = own
    def column(d):
        c = np.zeros(P)
        c[bucket(max(d, 0))] = 1
        c[32] = math.log(reach(d)) if reach(d) else NEG
        return c
    parts["oh"] = np.stack([column(255 - m) for m in range(384)]
                           + [column(PAST - p) for p in sample_positions()] + [column(0)], 1)
    parts["ones"] = np.ones((P, P))
    parts["limit"] = np.tile(np.arange(1, 5) * SLOTS, (P, 1))
    at, off = {}, 0
    for k, v in parts.items():
        at[k] = (off, v.shape[1])
        off += v.shape[1]
    return np.concatenate(list(parts.values()), 1).astype(np.float32), at


CONST, CONST_AT = constants()
NCONST = CONST.shape[1]


def stream():
    s = [("xp", 0), ("mp", 0)] + [("win", i) for i in range(12)]
    for i in range(4):
        s += [("qb", i), ("wk", 2 * i), ("wk", 2 * i + 1), ("wmv", i)]
    s += [("wmk", i) for i in range(4)] + [("wv", b) for b in range(NS)]
    s += [("wout", i) for i in range(4)] + [("wmq", i) for i in range(4)]
    for i in MEM_PAIRS:
        s += [("mqb", i), ("mk", 2 * i), ("mk", 2 * i + 1)]
    s += [("mv", b) for b in range(NS)] + [("wmo", i) for i in range(4)]
    return s


STREAM = stream()
AT = {key: n for n, key in enumerate(STREAM)}
NPRE = len(STREAM)
FILL = {1: 0, 2: 1, 4: 2, 5: 3, 7: 4, 8: 5, 10: 6, 11: 7}
PER_EXPERT = 12
ESLOTS = 16
ROUND = 4 * PER_EXPERT


def decoder_layer(nc, x_prompt, x_sample, mem_prompt, cache_win_k, cache_win_v, state_conv, cache_mem_k,
                  cache_mem_v, rel_bias_table, w_in, w_conv, w_out, ln1_g, ln1_b, w_mem_q, w_mem_k, w_mem_v,
                  w_mem_o, ln2_g, ln2_b, w_router, b_router, w_gate_up, b_gate_up, w_down, b_down, ln3_g,
                  ln3_b, const, y_prompt, y_sample, o_wk, o_wv, o_conv, o_mk, o_mv, o_sk, o_sv, o_sconv):
    ctx = ExitStack()
    with ctx:
        def sem(name):
            return ctx.enter_context(nc.semaphore(name))

        ring = ctx.enter_context(nc.sbuf_tensor("ring", [P, RING, 2048], F32))
        LATE = 2 * AW + H * 256 + 2 * D + 2 * 512 + 2 * 512
        ARENA = 28590 - LATE
        arena = ctx.enter_context(nc.sbuf_tensor("arena", [P, ARENA], F32))
        with ExitStack() as early:
            x_split = early.enter_context(nc.sbuf_tensor("x_split", [P, 2, DC, T], F32R))
            w_split = early.enter_context(nc.sbuf_tensor("w_split", [P, 2, 2, 1024], F32R))
        assert 2 * DC * T + 4 * 1024 <= LATE
        late = ctx.enter_context(nc.sbuf_tensor("late", [P, LATE], F32))
        nswi = ctx.enter_context(nc.sbuf_tensor("nswi", [1, 4], I32))
        ps = ctx.enter_context(nc.psum_tensor("ps", [P, 8, 512], F32))
        psf = ps[:, :, :].rearrange("p b n -> p (b n)")
        scratch_bias = nc.dram_tensor("scratch_bias", [H, P, 384], F32, kind="Internal").ap()
        scratch_q = nc.dram_tensor("scratch_q", [NS, AW], F32, kind="Internal").ap()
        scratch_mq = nc.dram_tensor("scratch_mq", [NS, D], F32, kind="Internal").ap()
        scratch_self = nc.dram_tensor("scratch_self", [NS, H], F32, kind="Internal").ap()

        top = [0]

        def region(n):
            a = top[0]
            top[0] += n
            return a

        def view(a, *dims):
            n = int(np.prod(dims))
            v = arena[:, a:a + n] if a < ARENA else late[:, a - ARENA:a - ARENA + n]
            if len(dims) == 2:
                return v.rearrange("p (a b) -> p a b", a=dims[0])
            if len(dims) == 3:
                return v.rearrange("p (a b c) -> p a b c", a=dims[0], b=dims[1])
            return v

        a_const = region(NCONST)
        cst = view(a_const, NCONST)

        def con(name):
            a, n = CONST_AT[name]
            return cst[:, a:a + n]
        ident = con("ident")
        a_small = region(700)
        small = view(a_small, 700)
        cut = [0]

        def tiny(n):
            a = cut[0]
            cut[0] += n
            assert cut[0] <= 700
            return small[:, a:a + n]

        a_xT = region(DC * T)
        xT = view(a_xT, DC, T)
        a_xh = region(3 * D)
        xh = view(a_xh, 3, D)
        a_bgu = region(2 * D)
        bgu = view(a_bgu, 2 * D)
        a_proj = region(24 * T)
        proj = view(a_proj, 24, T)
        mqT = view(a_proj + Q0 * T, DC, T)
        ks_nat = view(a_proj, AW)
        vs_nat = view(a_proj + AW, AW)
        knat = view(a_proj + V0 * T, 2, AW)
        a_mix = region(DC * T)
        mixT = view(a_mix, DC, T)
        a_memT = region(DC * MT)
        memT = view(a_memT, DC, MT)
        memkT = view(a_memT, DC, MT)
        memk_nat = view(a_xh, 2, D)
        qs_nat = view(a_xh + 2 * D, D)
        a_ss = region(200)
        ssc = view(a_ss, 200)
        assert top[0] <= ARENA, (top[0], ARENA)
        top[0] = ARENA
        a_vnat = region(2 * AW)
        vnat = view(a_vnat, 2, AW)
        a_bias = region(H * 256)
        bias = view(a_bias, H, 256)
        a_memv = region(2 * D)
        memv = view(a_memv, 2, D)
        a_lg = region(2 * 512)
        lg = view(a_lg, 2, 512)
        a_pt = region(2 * 512)
        pt = view(a_pt, 2, 512)
        assert top[0] == ARENA + LATE
        x_hi, x_lo = ([x_split[:, i, c, :] for c in range(DC)] for i in range(2))
        w_hi, w_lo = ([w_split[:, b, i, :] for b in range(2)] for i in range(2))
        b_row = view(a_xh + D, 384)
        es = view(a_bias, 264)
        pts = view(a_bias + 264, 2, 128)
        selfw = view(a_bias + 264 + 256, 128)
        avs = view(a_bias + 264 + 384, 2, D)
        stT = tiny(2 * 16).rearrange("p (c n) -> p c n", c=2)
        us = tiny(2 * NS).rearrange("p (c b) -> p c b", c=2)
        ul = tiny(2 * 2).rearrange("p (c k) -> p c k", c=2)
        wc = tiny(6).rearrange("p (k c) -> p k c", k=3)
        gcol = [tiny(DC) for _ in range(2)]
        bcol = [tiny(DC) for _ in range(2)]
        mx, nm, sm, rs = (tiny(4).rearrange("p (a b) -> p a b", a=2) for _ in range(4))
        ssm = tiny(8)
        stats = tiny(36).rearrange("p (t n) -> p t n", t=3)
        mv = tiny(6).rearrange("p (t n) -> p t n", t=3)
        rstd = tiny(6).rearrange("p (t n) -> p t n", t=3)
        tab = tiny(H)
        tab8 = tiny(NS * H)
        bsm = tiny(2 * H).rearrange("p (c h) -> p c h", c=2)
        brc = tiny(1)
        bself = tiny(1)
        warm = tiny(2)
        sself = tiny(1)
        dself = tiny(H)
        a_low = a_small + cut[0]
        tiny(P)
        beforeb, onesb = (arena[:, a_low + 64 * i:a_low + 64 * i + 64].bitcast(BF16) for i in range(2))
        m0 = a_proj
        xTe = view(m0, DC, P)
        g2 = view(m0 + 1024, 512)
        u2 = view(m0 + 1536, 512)
        sg_ = view(m0 + 2048, 512)
        act_ = view(m0 + 2560, 512)
        actT = view(m0 + 3072, 4, P)
        yb = view(m0 + 3584, 2, 512)
        wr = view(m0 + 4608, DC, NX)
        g3 = view(m0 + 4864, 2, D)
        m1 = m0 + 4864 + 2 * D
        assert m1 + 768 + 2 * T + 2 * SLOTS <= a_mix + DC * T
        Sel = view(m1, 3, 2, SLOTS)
        SelG = view(m1 + 384, 3, 2, SLOTS)
        SelT = view(m1 + 768, 2, T)
        selE = view(m1 + 768 + 2 * T, 2, SLOTS)
        m2 = a_vnat
        lgt, gtm, eqm, cum, posm, gat, rex = (view(m2 + 96 * i, 3, NX) for i in (0, 1, 2, 3, 5, 6, 7))
        msk = view(m2 + 384, 48).bitcast(BF16).rearrange("p (t e) -> p t e", t=3)
        lgTs = view(m2 + 768, T)
        top8 = view(m2 + 768 + T, 3, 8)
        left, rsum = (view(m2 + 792 + T + 3 * i, 3) for i in range(2))
        cmax, over, lim4 = view(m2 + 798 + T, 1), view(m2 + 799 + T, 1), view(m2 + 800 + T, 4)
        assert 804 + T <= 2 * AW
        extra = [view(a, 2048) for a in (a_memT, a_memv, a_lg, a_bias + D)]
        yo = view(a_bias, 3, D)

        landed = [sem(f"landed{s}") for s in range(RING)]
        landed_extra = [sem(f"landed_extra{i}") for i in range(4)]
        s_const = sem("s_const")
        s_ident = sem("s_ident")
        s_x0 = sem("s_x0")
        s_par = sem("s_par")
        s_late = sem("s_late")
        s_g3 = sem("s_g3")
        s_stored = sem("s_stored")
        s_yst = sem("s_yst")
        s_kvst = sem("s_kvst")
        s_mst = sem("s_mst")
        s_zero = sem("s_zero")
        s_xT = sem("s_xT")
        s_xT_out = sem("s_xT_out")
        s_mT = sem("s_mT")
        s_mT_out = sem("s_mT_out")
        s_xhi = sem("s_xhi")
        s_xlo = sem("s_xlo")
        s_whi = sem("s_whi")
        s_wlo = sem("s_wlo")
        s_wused = sem("s_wused")
        s_bgu = sem("s_bgu")
        s_half = sem("s_half")
        s_dn = sem("s_dn")
        s_dn_out = sem("s_dn_out")
        s_bt = sem("s_bt")
        s_bt_out = sem("s_bt_out")
        s_bscr = sem("s_bscr")
        s_bias = sem("s_bias")
        s_nat = sem("s_nat")
        s_nat_out = sem("s_nat_out")
        s_qscr = sem("s_qscr")
        s_mq = [sem(f"s_mq{i}") for i in range(4)]
        s_kr2 = sem("s_kr2")
        s_ka = sem("s_ka")
        s_mr = sem("s_mr")
        s_alpha = sem("s_alpha")
        s_first = sem("s_first")
        s_yz = sem("s_yz")
        s_spread = sem("s_spread")
        s_conv = sem("s_conv")
        s_sc = sem("s_sc")
        s_nm = sem("s_nm")
        s_ex = sem("s_ex")
        s_pn = sem("s_pn")
        s_pt = sem("s_pt")
        s_pt_out = sem("s_pt_out")
        s_av = sem("s_av")
        s_av_out = sem("s_av_out")
        s_kq = sem("s_kq")
        s_kr = sem("s_kr")
        s_mkT = sem("s_mkT")
        s_mkT_out = sem("s_mkT_out")
        s_ss = sem("s_ss")
        s_sT = sem("s_sT")
        s_snm = sem("s_snm")
        s_sex = sem("s_sex")
        s_spn = sem("s_spn")
        s_spT = sem("s_spT")
        s_spT_out = sem("s_spT_out")
        s_sav = sem("s_sav")
        s_sav_out = sem("s_sav_out")
        s_sat = sem("s_sat")
        s_sat_out = sem("s_sat_out")
        s_selfw = sem("s_selfw")
        s_selfd = sem("s_selfd")
        s_ln = sem("s_ln")
        s_var = sem("s_var")
        s_sq = sem("s_sq")
        s_xh = sem("s_xh")
        s_lt = sem("s_lt")
        s_lt_out = sem("s_lt_out")
        s_lt_odd = sem("s_lt_odd")
        s_x2 = sem("s_x2")
        s_x2_out = sem("s_x2_out")
        s_rt = sem("s_rt")
        s_rt_out = sem("s_rt_out")
        s_gex = sem("s_gex")
        s_low = sem("s_low")
        s_nsw = sem("s_nsw")
        s_yo = sem("s_yo")
        s_g3d = sem("s_g3d")
        dve_own = sem("dve_own")
        e_sel = sem("e_sel")
        e_selg = sem("e_selg")
        e_sb = sem("e_sb")
        e_gx = sem("e_gx")
        e_gx_out = sem("e_gx_out")
        e_wu = sem("e_wu")
        e_gu = sem("e_gu")
        e_g2 = sem("e_g2")
        e_u2 = sem("e_u2")
        e_sig = sem("e_sig")
        e_mul = sem("e_mul")
        e_act = sem("e_act")
        e_at = sem("e_at")
        e_at_out = sem("e_at_out")
        e_du = sem("e_du")
        e_dn = sem("e_dn")
        e_yb = sem("e_yb")
        s_yb_last = sem("s_yb_last")
        s_y1 = sem("s_y1")
        e_st = sem("e_st")
        e_st_out = sem("e_st_out")
        e_y = sem("e_y")
        e_y_out = sem("e_y_out")
        e_pos = sem("e_pos")

        def loads(n):
            return {"wk": 3, "wv": 3, "qb": 0, "mqb": 0}.get(STREAM[n][0], 1)

        def landed_at(n):
            return 16 * sum(loads(m) for m in range(n % RING, n + 1, RING))

        LBASE = [16 * sum(loads(m) for m in range(s, NPRE, RING)) for s in range(RING)]

        def arrived(eng, key):
            n = AT[key]
            if key[0] in ("qb", "mqb"):
                if key[0] == "qb":
                    eng.wait_ge(s_spread, 16 * (key[1] + 1))
                else:
                    eng.wait_ge(s_mq[key[1]], 16)
                return
            eng.wait_ge(landed[n % RING], landed_at(n))

        def slot(key):
            return ring[:, AT[key] % RING, :]

        def quarters(key):
            return slot(key).rearrange("p (k n) -> p k n", k=4)

        def halves(key):
            return slot(key).rearrange("p (k n) -> p k n", k=2)

        DENSE = ["win"] * 6 + ["wmv"] * 2 + ["wmk"] * 2 + ["wout"] * 2 + ["wmq"] * 2 + ["wmo"] * 2
        GROUP0 = {w: DENSE.index(w) for w in ("win", "wmv", "wmk", "wout", "wmq", "wmo")}
        TILE0 = {"win": 0, "wmv": 24, "wmk": 28, "wout": 32, "wmq": 40, "wmo": 48}

        def reader_done(eng, n):
            what, i = STREAM[n]
            if what == "xp":
                eng.wait_ge(s_xT, DC)
            elif what == "mp":
                eng.wait_ge(s_mT, DC)
            elif what == "win":
                eng.wait_ge(s_wlo, 2 * i + 2)
            elif what in GROUP0:
                if i % 2 == 0:
                    eng.wait_ge(s_half, GROUP0[what] + i // 2 + 1 - GROUP0["wmv"])
                else:
                    per = 2 if what in ("wmv", "wmk") else 4
                    eng.wait_ge(s_dn, TILE0[what] + per * (i // 2 + 1))
            elif what == "qb":
                eng.wait_ge(s_kq, 2 * i + 2)
            elif what == "wk":
                eng.wait_ge(s_kr, i + 1)
            elif what == "mqb":
                by_dve, by_pool = ([o.index(b) for b in (2 * i, 2 * i + 1) if b in o] for o in (BY_DVE, BY_POOL))
                if by_dve:
                    eng.wait_ge(s_kr2, max(by_dve) + 1)
                if by_pool:
                    eng.wait_ge(s_kq, NS + max(by_pool) + 1)
            elif what == "mk":
                if i in BY_ACT:
                    eng.wait_ge(s_ka, BY_ACT.index(i) + 1)
                else:
                    summed = BY_DVE + tuple(b for b in BY_POOL if b not in BY_ACT)
                    eng.wait_ge(s_kr2, summed.index(i) + 1)
            else:
                eng.wait_ge(s_sav, i // 4 + 1 + (2 if what == "mv" else 0))

        def expert_slot(m):
            m %= ESLOTS
            return extra[m] if m < 4 else ring[:, (NPRE + m - 4) % RING, :]

        def expert_landed(m):
            m %= ESLOTS
            return landed_extra[m] if m < 4 else landed[(NPRE + m - 4) % RING]

        def item_arrived(eng, r, m):
            base = 0 if m % ESLOTS < 4 else LBASE[(NPRE + m % ESLOTS - 4) % RING]
            eng.wait_ge(expert_landed(m), 48 * r + (16 * (m // ESLOTS) + 16 + base))

        def win_piece(p):
            return slot(("win", p // 2))[:, 1024 * (p % 2):1024 * (p % 2) + 1024]

        def piece_used(eng, p):
            if p % 4 == 3:
                eng.wait_ge(s_dn, p + 1)
            else:
                eng.wait_ge(s_wused, 3 * (p // 4) + p % 4 + 1)

        WPIECES = 2 * 12
        gate_rows = w_gate_up[0]
        down_rows = w_down[0]
        pos = sample_positions()
        assert pos == list(range(0, 512, 16)) + list(range(512, 896, 4)) + list(range(896, PAST))

        block = ctx.enter_context(nc.Block())

        @block.sync
        def _(sp):
            sp.dma_start(ident, const[:, 0:P]).then_inc(s_ident, 16)
            for j in range(2):
                sp.dma_start(halves(("xp", 0))[:, :, 512 * j:512 * j + 512],
                             x_prompt[0].rearrange("(k p) n -> p k n", p=P)[:, :, 512 * j:512 * j + 512]).then_inc(
                                 s_x0 if j == 0 else landed[0], 16)
                if j == 0:
                    sp.dma_start(xh[0:NS, 2, :], x_sample.rearrange("b s d -> (b s) d")).then_inc(s_ident, 16)
            sp.dma_start(cst[:, P:NCONST], const[:, P:NCONST]).then_inc(s_const, 16)
            sp.dma_start(tab[0:NX, :], rel_bias_table).then_inc(s_const, 16)
            sp.dma_start(xh[0:2 * NS, 0, 0:CW], state_conv[0].rearrange("b k c -> (b k) c")).then_inc(s_const, 16)
            for n, (what, i) in enumerate(STREAM):
                if n == 0 or what in ("qb", "mqb"):
                    continue
                if n >= RING:
                    reader_done(sp, n - RING)
                done = landed[n % RING]
                two = ring[:, n % RING, :].rearrange("p (k n) -> p k n", k=2)
                if what == "mp":
                    sp.dma_start(two, mem_prompt[0].rearrange("(k p) n -> p k n", p=P)).then_inc(done, 16)
                elif what in GROUP0:
                    w = {"win": w_in, "wmk": w_mem_k, "wmv": w_mem_v, "wout": w_out, "wmq": w_mem_q,
                         "wmo": w_mem_o}[what][0]
                    r0, c0 = 512 * (i % 2), 512 * (i // 2)
                    sp.dma_start(ring[:, n % RING, :].rearrange("p (k n) -> p k n", k=4),
                                 w[r0:r0 + 512, c0:c0 + 512].rearrange("(k p) n -> p k n", p=P)).then_inc(done, 16)
                elif what in ("wk", "wv"):
                    c = (cache_win_k if what == "wk" else cache_win_v)[0, i].rearrange("s h e -> s (h e)")
                    sp.dma_start(two[0:32, 0, 0:AW],
                                 c[0:512].rearrange("(s r) n -> s r n", r=16)[:, 0, :]).then_inc(done, 16)
                    sp.dma_start(two[32:P, 0, 0:AW],
                                 c[512:896].rearrange("(s r) n -> s r n", r=4)[:, 0, :]).then_inc(done, 16)
                    sp.dma_start(two[:, 1, 0:AW], c[896:PAST]).then_inc(done, 16)
                else:
                    c = (cache_mem_k if what == "mk" else cache_mem_v)[0, i].rearrange("m h e -> m (h e)")
                    sp.dma_start(two, c.rearrange("(k p) n -> p k n", p=P)).then_inc(done, 16)

            def item_load(e0, m):
                e, i = e0 + m // PER_EXPERT, m % PER_EXPERT
                dst, done = expert_slot(m), expert_landed(m)
                if i < 8:
                    src = gate_rows[bass.ds(e, 1), i * P:(i + 1) * P, :].rearrange("a p n -> (a p) n")
                    sp.dma_start(dst, src).then_inc(done, 16)
                else:
                    src = down_rows[bass.ds(e, 1), (i - 8) * 2 * P:(i - 7) * 2 * P, :].rearrange(
                        "a (k p) n -> p (a k) n", p=P)
                    sp.dma_start(dst.rearrange("p (k n) -> p k n", k=2), src).then_inc(done, 16)

            def item_read(k0, m):
                k, i = k0 + m // PER_EXPERT, m % PER_EXPERT
                if i < 7:
                    sp.wait_ge(e_wu, 7 * k + (i + 1))
                elif i == 7:
                    sp.wait_ge(e_gu, k + 1)
                elif i < 11:
                    sp.wait_ge(e_du, 3 * k + (i - 7))
                else:
                    sp.wait_ge(e_dn, k + 1)

            def round_loads(e0, before):
                for m in range(ROUND):
                    if m < ESLOTS:
                        item_read(before, m + ROUND - ESLOTS)
                    else:
                        item_read(before + 4, m - ESLOTS)
                    item_load(e0, m)

            sp.wait_ge(s_sc, H + MH)
            item_load(0, 0)
            sp.wait_ge(s_av, H + MH)
            sp.wait_ge(s_mst, 32)
            item_load(0, 1)
            item_load(0, 2)
            sp.wait_ge(s_sat, 4)
            item_load(0, 3)
            for i in range(RING):
                reader_done(sp, NPRE + i - RING)
                item_load(0, 4 + i)
            for m in range(ESLOTS, ROUND):
                item_read(0, m - ESLOTS)
                item_load(0, m)
            with sp.Fori(1, NX // 4) as r:
                round_loads(r * 4, (r - 1) * 4)
            sp.wait_ge(s_nsw, 4)
            rounds = sp.value_load(nswi[0:1, 1:2], min_val=8, max_val=40)
            with sp.If(rounds > NX // 4):
                with sp.Fori(NX // 4, rounds) as r:
                    round_loads((r % 8) * 4, (r - 1) * 4)
            yp = y_prompt[0].rearrange("(k p) n -> p k n", p=P)
            for t in (LORDER[1], LORDER[0], LORDER[2]):
                if t == LORDER[0]:
                    sp.wait_ge(s_y1, 2)
                else:
                    sp.wait_ge(s_yo, 1 if t == LORDER[1] else 2)
                if t < 2:
                    sp.dma_start(yp[:, t, :], yo[:, t, :]).then_inc(s_yst, 16)
                else:
                    sp.dma_start(y_sample.rearrange("b s d -> (b s) d"), yo[0:NS, 2, :]).then_inc(s_yst, 16)
            sp.wait_ge(s_yst, 16 * 3)
            sp.wait_ge(s_stored, 16 * 5)
            sp.wait_ge(s_kvst, 16 * 4)
            sp.wait_ge(s_mst, 16 * 2)

        @block.gpsimd
        def _(pool):
            nc.gpsimd.memset(tab[NX:NX + 1, :], 1.0).then_inc(s_zero, 1)
            pool.wait_ge(s_zero, 1)
            nc.gpsimd.memset(bgu, 0.0).then_inc(s_zero, 1)
            pool.wait_ge(s_const, 48)
            pool.wait_ge(s_zero, 2)
            nc.gpsimd.tensor_copy(tab8[0:NX + 1, :].rearrange("p (b h) -> p b h", b=NS),
                                  tab[0:NX + 1, :].unsqueeze(1).broadcast_to((NX + 1, NS, H))).then_inc(s_zero, 1)
            with nc.allow_non_contiguous_dma(reason="columns of small parameters"):
                for k in range(3):
                    pool.dma_start(wc[:, k, :], w_conv[0, k].rearrange("(c p) -> p c", p=P)).then_inc(s_par, 16)
                for g, b, gc, bc in ((ln1_g, ln1_b, gcol[0], bcol[0]), (ln2_g, ln2_b, gcol[1], bcol[1])):
                    pool.dma_start(gc, g[0].rearrange("(c p) -> p c", p=P)).then_inc(s_par, 16)
                    pool.dma_start(bc, b[0].rearrange("(c p) -> p c", p=P)).then_inc(s_par, 16)
                pool.dma_start(brc[0:NX, :], b_router[0].rearrange("(e a) -> e a", a=1)).then_inc(s_par, 16)
            pool.dma_start(bgu[0:NX, :], b_gate_up[0]).then_inc(s_bgu, 16)
            pool.dma_start(o_sconv[0, :, 0, :], state_conv[0, :, 1, :]).then_inc(s_stored, 16)
            pool.wait_ge(s_bt_out, 1)
            pool.dma_start(scratch_bias, b_row[0:H, :].unsqueeze(1).broadcast_to((H, P, 384))).then_inc(s_bscr, 16)

            def spread(kind, src, width, i, done):
                n = AT[(kind, i)]
                reader_done(pool, n - RING)
                dst = ring[:, n % RING, 0:2 * width].rearrange("p (b n) -> p b n", b=2)
                pool.dma_start(dst, src[2 * i:2 * i + 2].unsqueeze(0).broadcast_to((P, 2, width))).then_inc(
                    done, 16)

            def products(kq, kk, width, b):
                arrived(pool, (kq, b // 2))
                arrived(pool, (kk, b))
                q = slot((kq, b // 2))[:, (b % 2) * width:(b % 2 + 1) * width]
                k = halves((kk, b))[:, :, 0:width]
                nc.gpsimd.tensor_tensor(k, k, q.unsqueeze(1).broadcast_to((P, 2, width)), ALU.mult).then_inc(
                    s_kq, 1)

            pool.wait_ge(s_nat_out, 1)
            pool.dma_start(scratch_q, qs_nat[0:NS, 0:AW]).then_inc(s_qscr, 16)
            pool.wait_ge(s_qscr, 16)
            for b in range(NS):
                if b % 2 == 0:
                    spread("qb", scratch_q, AW, b // 2, s_spread)
                products("qb", "wk", AW, b)
            pool.wait_ge(s_nat_out, 7)
            rows = lambda o: o[0, 0].rearrange("s h e -> s (h e)").rearrange("(k p) n -> p k n", p=P)
            flat = lambda o: o[0, :, 0].rearrange("b h e -> b (h e)")
            pool.dma_start(rows(o_wv), vnat).then_inc(s_kvst, 16)
            pool.dma_start(rows(o_wk), knat).then_inc(s_kvst, 16)
            pool.dma_start(flat(o_sk), ks_nat[0:NS, :]).then_inc(s_kvst, 16)
            pool.dma_start(flat(o_sv), vs_nat[0:NS, :]).then_inc(s_kvst, 16)
            with nc.allow_non_contiguous_dma(reason="conv rows, one element per channel"):
                for c in range(2):
                    pool.dma_start(o_conv[0, 0].rearrange("k (c p) -> p c k", p=P)[:, c, :],
                                   ul[:, c, :]).then_inc(s_stored, 16)
                    pool.dma_start(o_sconv[0, :, 1, :].rearrange("b (c p) -> p c b", p=P)[:, c, :],
                                   us[:, c, :]).then_inc(s_stored, 16)
            pool.wait_ge(s_selfd, 1)
            pool.dma_start(scratch_self, dself[0:NS, :]).then_inc(s_selfw, 16)
            pool.wait_ge(s_selfw, 16)
            with nc.allow_non_contiguous_dma(reason="one score per row"):
                pool.dma_start(sself[0:NS * H, 0:1], scratch_self.rearrange("b (h a) -> (b h) a", a=1)).then_inc(
                    s_selfw, 16)
            mrows = lambda o: o[0, 0].rearrange("m h e -> m (h e)").rearrange("(k p) n -> p k n", p=P)
            pool.wait_ge(s_dn_out, 32)
            pool.dma_start(mrows(o_mv), memv).then_inc(s_mst, 16)
            pool.dma_start(mrows(o_mk), memk_nat).then_inc(s_mst, 16)
            pool.wait_ge(s_nat_out, 8)
            pool.dma_start(scratch_mq, qs_nat[0:NS, :]).then_inc(s_qscr, 16)
            pool.wait_ge(s_qscr, 32)
            for i in MEM_PAIRS:
                spread("mqb", scratch_mq, D, i, s_mq[i])
            for b in BY_POOL:
                products("mqb", "mk", D, b)
            pool.wait_ge(s_kvst, 64)
            pool.dma_start(wr, w_router[0].rearrange("(c p) e -> p c e", p=P)).then_inc(s_late, 16)
            pool.wait_ge(s_dn, 56)
            pool.dma_start(g3[:, 0, :], ln3_g.broadcast_to((P, D))).then_inc(s_g3, 16)
            pool.dma_start(g3[:, 1, :], ln3_b.broadcast_to((P, D))).then_inc(s_g3, 16)
            pool.wait_ge(s_yz, 1)
            pool.dma_start(yb[0:NX], b_down[0].rearrange("e (h n) -> e h n", h=2)).then_inc(s_first, 16)
            y1 = yo[:, LORDER[0], :]
            pool.wait_ge(s_g3, 32)
            pool.wait_ge(s_xh, 7)
            nc.gpsimd.tensor_tensor(y1, y1, g3[:, 0, :], ALU.mult).then_inc(s_y1, 1)
            pool.wait_ge(s_y1, 1)
            nc.gpsimd.tensor_tensor(y1, y1, g3[:, 1, :], ALU.add).then_inc(s_y1, 1)

        @block.scalar
        def _(act):
            for c in range(DC):
                act.wait_ge(s_xT, c + 1)
                nc.scalar.copy(xT[:, c, :], ps[:, c % 4, 0:T]).then_inc(s_xT_out, 1)
                act.wait_ge(s_xT_out, c + 1)
                nc.scalar.copy(x_hi[c], xT[:, c, :]).then_inc(s_xhi, 1)

            def dense_out(n, dst, width, scale=1.0):
                act.wait_ge(s_dn, n + 1)
                nc.scalar.activation(dst, ps[:, n % 4, 0:width], ACT.Copy, scale=scale).then_inc(s_dn_out, 1)

            def high_part(p):
                if p >= WPIECES:
                    return
                if p % 2 == 0:
                    arrived(act, ("win", p // 2))
                if p >= 2:
                    piece_used(act, p - 2)
                nc.scalar.copy(w_hi[p % 2], win_piece(p)).then_inc(s_whi, 1)

            high_part(0)
            for g in range(6):
                for p in range(4 * g, 4 * g + 4):
                    high_part(p + 1)
                for n in range(4 * g, 4 * g + 4):
                    dense_out(n, proj[:, n, :], T, 0.125 if Q0 <= n < K0 else 1.0)
            act.wait_ge(s_bscr, 16)
            act.dma_start(bias, bass.AP(scratch_bias.tensor, P - 1, [[383, P], [P * 384, H], [1, 256]])).then_inc(
                s_bias, 16)

            def expo(h, wide_):
                act.wait_ge(s_nm, h + 1)
                b = h % 2
                parts = ((0, 256), (256, 512)) if wide_ else ((0, 128), (128, 384))
                for c, (a, z) in enumerate(parts):
                    src = ps[:, 4 + b, a:z] if wide_ else lg[:, b, a:z]
                    nc.scalar.activation(lg[:, b, a:z], src, ACT.Exp, bias=nm[:, b, c:c + 1],
                                         accum_out=sm[:, b, c:c + 1]).then_inc(s_ex, 1)

            def pt_out(h, n):
                act.wait_ge(s_pt, h + 1)
                if h >= 2:
                    act.wait_ge(s_av, h - 1)
                nc.scalar.copy(pt[:, h % 2, 0:n], ps[:, 6, 0:n]).then_inc(s_pt_out, 1)

            def av_out(h):
                act.wait_ge(s_av, h + 1)
                r = E * (h % 2)
                nc.scalar.copy(mixT[r:r + E, 2 + h // 2, 0:NP_], ps[r:r + E, 7, 0:NP_]).then_inc(s_av_out, 1)

            for step in range(H + 2):
                if step < H:
                    expo(step, False)
                if 1 <= step <= H:
                    pt_out(step - 1, 384)
                if step >= 2:
                    av_out(step - 2)
                f = FILL.get(step)
                if f is not None and f % 2 == 1:
                    g = f // 2
                    for m in range(2):
                        n = 24 + 2 * g + m
                        dst = (memv if g < 2 else memk_nat)[:, m, 512 * (g % 2):512 * (g % 2) + 512]
                        dense_out(n, dst, 512)

            def sample_exp(k, n, own_score):
                act.wait_ge(s_snm, k + 1)
                nc.scalar.activation(es[0:n, 0:256], ps[0:n, 4, 0:256], ACT.Exp, bias=ssm[0:n, 2:3],
                                     accum_out=ssm[0:n, 3:4]).then_inc(s_sex, 1)
                if own_score:
                    nc.scalar.activation(es[0:n, 256:257], ssm[0:n, 0:1], ACT.Exp,
                                         bias=ssm[0:n, 2:3]).then_inc(s_sex, 1)

            def sample_av_out(k, width):
                for g in range(2):
                    act.wait_ge(s_sav, 2 * k + g + 1)
                    nc.scalar.copy(avs[:, g, 0:width], psf[:, 2048 + 1024 * g:2048 + 1024 * g + width]).then_inc(
                        s_sav_out, 1)

            def layer_norm(k):
                for t, (_, n) in enumerate(TCH):
                    act.wait_ge(s_var, 3 * k + t + 1)
                    nc.scalar.activation(rstd[0:n, t, 0:1], rstd[0:n, t, 0:1], ACT.Sqrt).then_inc(s_sq, 1)
                    act.wait_ge(s_mr, 3 * k + t + 1)
                    nc.scalar.activation(xh[0:n, t, :], psf[0:n, 512 * ROWB[t]:512 * ROWB[t] + D], ACT.Identity,
                                         bias=mv[0:n, t, 1:2], scale=rstd[0:n, t, 1:2]).then_inc(s_xh, 1)
                for c in range(0, DC, 2):
                    act.wait_ge(s_lt, DC * k + c + 1)
                    nc.scalar.activation(xT[:, c, :], ps[:, 2 + c % 4, 0:T], ACT.Identity, bias=bcol[k][:, c:c + 1],
                                         scale=gcol[k][:, c:c + 1]).then_inc(s_lt_out, 1)

            def last_layer_norm():
                for i, t in enumerate(LORDER):
                    n = TCH[t][1]
                    act.wait_ge(s_var, 6 + i + 1)
                    nc.scalar.activation(rstd[0:n, t, 0:1], rstd[0:n, t, 0:1], ACT.Sqrt).then_inc(s_sq, 1)
                    if i == 0:
                        act.wait_ge(s_mr, 6 + 1)
                        nc.scalar.activation(yo[0:n, t, :], psf[0:n, 512 * LASTB[t]:512 * LASTB[t] + D],
                                             ACT.Identity, bias=mv[0:n, t, 1:2], scale=rstd[0:n, t, 1:2]).then_inc(
                                                 s_xh, 1)

            def key_sum(b):
                act.wait_ge(s_kq, NS + BY_POOL.index(b) + 1)
                for c in range(2):
                    for h in range(MH):
                        v = halves(("mk", b))[:, c, MT * h:MT * h + MT]
                        to = (c * NS + b) * MH + h
                        ins = nc.scalar.activation(v, v, ACT.Copy, accum_out=ssc[:, to:to + 1])
                ins.then_inc(s_ka, 1)

            sample_exp(0, NS * H, True)
            sample_av_out(0, AW)
            nc.scalar.activation(warm[:, 0:1], con("ones")[:, 0:1], ACT.Sqrt)
            act.wait_ge(s_par, 16 * 8)
            act.wait_ge(s_mst, 32)
            layer_norm(0)
            for n in range(40, 48):
                dense_out(n, mqT[:, n - 40, :], T, 1.0 / 16)
            for h in range(H, H + MH + 2):
                if h < H + MH:
                    expo(h, True)
                if H + 1 <= h <= H + MH:
                    pt_out(h - 1, 512)
                if h >= H + 2:
                    act.wait_ge(s_av, h - 1)
                    j = h - 2 - H
                    nc.scalar.copy(mixT[:, 2 * j:2 * j + 2, 0:NP_],
                                   ps[:, 7, :].rearrange("p (c n) -> p c n", c=2)).then_inc(s_av_out, 1)
                if h >= H + MH - 1 and h < H + MH - 1 + len(BY_ACT):
                    key_sum(BY_ACT[h - (H + MH - 1)])
            sample_exp(1, NS * MH, False)
            sample_av_out(1, D)
            nc.scalar.activation(warm[:, 1:2], con("ones")[:, 0:1], ACT.Sqrt)
            layer_norm(1)
            for t, (_, n) in enumerate(TCH):
                act.wait_ge(s_x2, t + 1)
                b = (4, 6, 2)[t]
                nc.scalar.copy(xh[0:n, t, :], psf[0:n, 512 * b:512 * b + D]).then_inc(s_x2_out, 1)
            act.wait_ge(s_rt_out, 3)
            nc.scalar.activation(rex, rex, ACT.Exp).then_inc(s_gex, 1)

            act.wait_ge(s_nsw, 4)
            act.sem_inc(e_yb, 1)
            act.sem_inc(e_at_out, 1)
            pairs_but_one = act.value_load(nswi[0:1, 3:4], min_val=15, max_val=79)
            act.wait_ge(e_gx, 1)
            nc.scalar.copy(xTe, ps[:, 6:8, :].rearrange("p b (c n) -> p (b c) n", n=P)).then_inc(e_gx_out, 1)

            def pair(it, last=False):
                for a in range(2):
                    act.wait_ge(e_g2, 2 * it + (a + 1))
                    nc.scalar.activation(sg_, g2, ACT.Sigmoid, scale=1.702).then_inc(e_sig, 1)
                    if a == 1 and not last:
                        act.wait_ge(e_gx, it + 2)
                        nc.scalar.copy(xTe, ps[:, 6:8, :].rearrange("p b (c n) -> p (b c) n", n=P)).then_inc(
                            e_gx_out, 1)
                    act.wait_ge(e_at, 2 * it + (a + 2))
                    nc.scalar.copy(actT, ps[:, 2, :].rearrange("p (q n) -> p q n", q=4)).then_inc(e_at_out, 1)
                act.wait_ge(e_dn, 2 * it + 2)
                if last:
                    nc.scalar.copy(yb[:, 0, :], ps[:, 4, :]).then_inc(e_yb, 1)
                else:
                    nc.scalar.copy(yb, ps[:, 4:6, :]).then_inc(e_yb, 1)

            with act.Fori(0, pairs_but_one) as it:
                pair(it)
            pair(pairs_but_one, last=True)
            last_layer_norm()

        @block.vector
        def _(dve):
            own = [0]

            def link(ins):
                own[0] += 1
                ins.then_inc(dve_own, 1)
                dve.wait_ge(dve_own, own[0])

            dve.wait_ge(s_const, 48)
            def low_parts(p0, p1):
                for p in range(p0, p1):
                    if p % 2 == 0:
                        arrived(dve, ("win", p // 2))
                    dve.wait_ge(s_whi, p + 1)
                    if p >= 2:
                        piece_used(dve, p - 2)
                    nc.vector.tensor_tensor(w_lo[p % 2], win_piece(p), w_hi[p % 2].bitcast(F32),
                                            ALU.subtract).then_inc(s_wlo, 1)

            for c in range(DC):
                dve.wait_ge(s_xhi, c + 1)
                nc.vector.tensor_tensor(x_lo[c], xT[:, c, :], x_hi[c].bitcast(F32), ALU.subtract).then_inc(s_xlo, 1)
            for c in range(DC):
                dve.wait_ge(s_mT, c + 1)
                nc.vector.tensor_copy(memT[:, c, :], ps[:, 4 + c % 4, 0:MT]).then_inc(s_mT_out, 1)
            low_parts(0, 2)
            dve.wait_ge(s_bt, 1)
            nc.vector.tensor_copy(b_row[0:H, :], ps[0:H, 4, 0:384]).then_inc(s_bt_out, 1)
            nc.vector.tensor_copy(bsm, ps[:, 5, 0:2 * H].rearrange("p (c h) -> p c h", c=2)).then_inc(s_bt_out, 1)
            nc.vector.tensor_copy(bself[0:NS * H, :], ps[0:NS * H, 5, 32:33]).then_inc(s_bt_out, 1)
            nc.vector.tensor_copy(stT, ps[:, 6, 0:32].rearrange("p (c n) -> p c n", c=2)).then_inc(s_bt_out, 1)
            def rows_out(k, dst, n, width):
                b = (4, 4, 6, 4, 6, 4, 6)[k] if k < 7 else 4
                dve.wait_ge(s_nat, k + 1)
                nc.vector.tensor_copy(dst, psf[0:n, 512 * b:512 * b + width]).then_inc(s_nat_out, 1)

            low_parts(2, 16)
            rows_out(0, qs_nat[0:NS, 0:AW], NS, AW)
            low_parts(16, 18)

            dve.wait_ge(s_dn_out, 6)
            dve.wait_ge(s_par, 16 * 8)
            dve.wait_ge(s_bt_out, 4)
            u = proj[:, GC0:GC0 + 2, :]
            link(nc.vector.tensor_tensor(u, u, proj[:, HH0:HH0 + 2, :], ALU.mult))
            nc.vector.tensor_copy(us, u[:, :, NP_:T]).then_inc(s_conv, 1)
            nc.vector.tensor_copy(ul, u[:, :, NP_ - 2:NP_]).then_inc(s_conv, 1)
            link(nc.vector.tensor_scalar(mixT[:, 0, :], u[:, 0, :], wc[:, 2, 0:1], None, ALU.mult))
            low_parts(18, 19)
            link(nc.vector.tensor_scalar(mixT[:, 1, :], u[:, 1, :], wc[:, 2, 1:2], None, ALU.mult))
            for tap, back in ((1, 1), (0, 2)):
                for c in range(2):
                    o = mixT[:, c, back:NP_]
                    link(nc.vector.scalar_tensor_tensor(o, u[:, c, 0:NP_ - back], wc[:, tap, c:c + 1], o,
                                                        ALU.mult, ALU.add))
                    o = mixT[:, c, NP_:T]
                    st = stT[:, c, :].rearrange("p (b k) -> p k b", k=2)[:, tap, :]
                    link(nc.vector.scalar_tensor_tensor(o, st, wc[:, tap, c:c + 1], o, ALU.mult, ALU.add))
                low_parts(20 - tap, 21 - tap)
            link(nc.vector.tensor_tensor(mixT[:, 0:2, :], mixT[:, 0:2, :], proj[:, GB0:GB0 + 2, :], ALU.mult))

            low_parts(21, WPIECES)
            nc.vector.tensor_copy(beforeb, con("before")).then_inc(s_low, 1)
            nc.vector.tensor_copy(onesb, con("ones")).then_inc(s_low, 1)
            rows_out(1, vnat[:, 0, :], P, AW)
            rows_out(2, vnat[:, 1, :], P, AW)
            rows_out(3, vs_nat[0:NS, :], NS, AW)
            rows_out(4, knat[:, 0, :], P, AW)
            rows_out(5, knat[:, 1, :], P, AW)
            rows_out(6, ks_nat[0:NS, :], NS, AW)
            dve.wait_ge(s_nat_out, 7)
            dve.wait_ge(s_qscr, 16)
            q_s = qs_nat[0:NS, 0:AW]
            link(nc.vector.tensor_tensor(q_s, q_s, ks_nat[0:NS, :], ALU.mult))
            nc.vector.tensor_reduce(dself[0:NS, :], q_s.rearrange("p (h e) -> p h e", h=H), AX.X, ALU.add).then_inc(
                s_selfd, 1)

            def head_max(h):
                b = h % 2
                dve.wait_ge(s_sc, h + 1)
                if h == 0:
                    dve.wait_ge(s_bias, 16)
                if h >= 2:
                    dve.wait_ge(s_pt, h - 1)
                for c, (a, z, w) in enumerate(((0, 128, 128), (128, 384, 0))):
                    nc.vector.tensor_tensor_reduce(lg[:, b, a:z], ps[:, 4 + b, a:z], bias[:, h, w:256], 1.0, -3e38,
                                                   ALU.add, ALU.max, mx[:, b, c:c + 1]).then_inc(dve_own, 1)
                    own[0] += 1
                dve.wait_ge(dve_own, own[0])
                nc.vector.tensor_scalar(nm[:, b, :], mx[:, b, :], -1.0, None, ALU.mult).then_inc(s_nm, 1)

            def head_norm(h, parts):
                b = h % 2
                dve.wait_ge(s_ex, 2 * h + 2)
                link(nc.vector.reciprocal(rs[:, b, :], sm[:, b, :]))
                for c, (a, z) in enumerate(parts):
                    ins = nc.vector.tensor_scalar(lg[:, b, a:z], lg[:, b, a:z], rs[:, b, c:c + 1], None, ALU.mult)
                    ins.then_inc(s_pn, 1)

            def key_sums(kk, width, heads, b, n_products, done):
                dve.wait_ge(s_kq, n_products)
                n = width // heads
                src = halves((kk, b))[:, :, 0:width].rearrange("p c (h e) -> p c h e", e=n)
                dst = ssc[:, 0:2 * NS * heads].rearrange("p (c b h) -> p c b h", c=2, b=NS)[:, :, b, :]
                nc.vector.tensor_reduce(dst, src, AX.X, ALU.add).then_inc(done, 1)

            def key_scores(b):
                arrived(dve, ("mqb", b // 2))
                arrived(dve, ("mk", b))
                for c in range(2):
                    for h in range(MH):
                        k = halves(("mk", b))[:, c, MT * h:MT * h + MT]
                        q = slot(("mqb", b // 2))[:, (b % 2) * D + MT * h:(b % 2) * D + MT * h + MT]
                        to = (c * NS + b) * MH + h
                        ins = nc.vector.tensor_tensor_reduce(k, k, q, 1.0, 0.0, ALU.mult, ALU.add,
                                                             ssc[:, to:to + 1])
                ins.then_inc(s_kr2, 1)

            for step in range(H + 1):
                if step < H:
                    head_max(step)
                if 2 <= step < 2 + NS:
                    key_sums("wk", AW, H, step - 2, step - 1, s_kr)
                if step < H:
                    head_norm(step, ((0, 128), (128, 384)))

            for c in range(DC):
                dve.wait_ge(s_mkT, c + 1)
                nc.vector.tensor_copy(memkT[:, c, :], ps[:, 4 + c % 4, 0:MT]).then_inc(s_mkT_out, 1)

            def sample_softmax(k, heads):
                n = NS * heads
                if k == 0:
                    dve.wait_ge(s_selfw, 32)
                    link(nc.vector.tensor_tensor(sself[0:n, :], sself[0:n, :], bself[0:n, :], ALU.add))
                dve.wait_ge(s_sT, k + 1)
                link(nc.vector.tensor_reduce(ssm[0:n, 1:2], ps[0:n, 4, 0:256], AX.X, ALU.max))
                if k == 0:
                    link(nc.vector.tensor_copy(ssm[0:n, 0:1], sself[0:n, :]))
                    link(nc.vector.tensor_tensor(ssm[0:n, 1:2], ssm[0:n, 1:2], ssm[0:n, 0:1], ALU.max))
                nc.vector.tensor_scalar(ssm[0:n, 2:3], ssm[0:n, 1:2], -1.0, None, ALU.mult).then_inc(s_snm, 1)
                dve.wait_ge(s_sex, 2 if k == 0 else 3)
                if k == 0:
                    link(nc.vector.tensor_tensor(ssm[0:n, 3:4], ssm[0:n, 3:4], es[0:n, 256:257], ALU.add))
                link(nc.vector.reciprocal(ssm[0:n, 4:5], ssm[0:n, 3:4]))
                w = 257 if k == 0 else 256
                nc.vector.tensor_scalar(es[0:n, 0:w], es[0:n, 0:w], ssm[0:n, 4:5], None, ALU.mult).then_inc(s_spn, 1)
                link(nc.vector.memset(pts, 0.0))
                if k == 0:
                    link(nc.vector.memset(selfw, 0.0))
                dve.wait_ge(s_spT, k + 1)
                if k == 0:
                    nc.vector.tensor_tensor(selfw[0:NS, 0:n], ps[0:NS, 6, 0:n], con("own")[0:NS, :],
                                            ALU.mult).then_inc(s_spT_out, 1)
                nc.vector.tensor_copy(pts[:, :, 0:n], ps[:, 5, 0:2 * n].rearrange("p (c n) -> p c n", c=2)).then_inc(
                    s_spT_out, 1)

            def sample_pick(k):
                for g in range(2):
                    dve.wait_ge(s_sat, 2 * k + g + 1)
                    base = 2048 + 1024 * g
                    c0 = NP_ + 4 * g
                    for c in range(HP if k == 0 else DC):
                        lanes = psf[:, base + P * c:base + P * c + P].rearrange("p (l h) -> p h l", l=4)
                        if k == 0:
                            for i in range(2):
                                r = E * i
                                nc.vector.tensor_copy(mixT[r:r + E, 2 + c, c0:c0 + 4],
                                                      lanes[r:r + E, 2 * c + i, :]).then_inc(s_sat_out, 1)
                        else:
                            nc.vector.tensor_copy(mixT[:, c, c0:c0 + 4], lanes[:, c // 2, :]).then_inc(s_sat_out, 1)

            def residual(n0):
                for n in range(n0, n0 + DC):
                    dve.wait_ge(s_dn, n + 1)
                    x = xT[:, n - n0, :]
                    nc.vector.scalar_tensor_tensor(x, x, ALPHA, ps[:, n % 4, 0:T], ALU.mult, ALU.add).then_inc(
                        s_dn_out, 1)

            def stats_of(k, i, t, bank, between=lambda: None):
                n = TCH[t][1]
                dve.wait_ge(s_ln, 3 * k + i + 1)
                for j in range(2):
                    own[0] += 1
                    nc.vector.bn_stats(stats[0:n, t, 6 * j:6 * j + 6], ps[0:n, bank + j, :]).then_inc(dve_own, 1)
                    if j == 0:
                        between()
                dve.wait_ge(dve_own, own[0])
                link(nc.vector.bn_aggr(mv[0:n, t, :], stats[0:n, t, :]))
                nc.vector.tensor_scalar(rstd[0:n, t, 0:1], mv[0:n, t, 1:2], EPS, None, ALU.add).then_inc(s_var, 1)

            def scale_of(k, i, t, shift):
                n = TCH[t][1]
                dve.wait_ge(s_sq, 3 * k + i + 1)
                link(nc.vector.reciprocal(rstd[0:n, t, 1:2], rstd[0:n, t, 0:1]))
                if shift:
                    nc.vector.scalar_tensor_tensor(mv[0:n, t, 1:2], mv[0:n, t, 0:1], -1.0, rstd[0:n, t, 1:2],
                                                   ALU.mult, ALU.mult).then_inc(s_mr, 1)

            def layer_norm(k):
                stats_of(k, 0, 0, ROWB[0])
                stats_of(k, 1, 1, ROWB[1], lambda: scale_of(k, 0, 0, True))
                stats_of(k, 2, 2, ROWB[2], lambda: scale_of(k, 1, 1, True))
                scale_of(k, 2, 2, True)
                for c in range(1, DC, 2):
                    dve.wait_ge(s_lt, DC * k + c + 1)
                    nc.vector.tensor_scalar(xT[:, c, :], ps[:, 2 + c % 4, 0:T], gcol[k][:, c:c + 1],
                                            bcol[k][:, c:c + 1], ALU.mult, ALU.add).then_inc(s_lt_odd, 1)

            def last_layer_norm():
                dve.wait_ge(s_g3, 32)
                for i, t in enumerate(LORDER):
                    n = TCH[t][1]
                    stats_of(2, i, t, LASTB[t])
                    if i:
                        nc.vector.scalar_tensor_tensor(
                            yo[0:n, t, :], psf[0:n, 512 * LASTB[t]:512 * LASTB[t] + D], mv[0:n, t, 0:1],
                            g3[0:n, 0, :], ALU.subtract, ALU.mult).then_inc(s_g3d, 1)
                    scale_of(2, i, t, i == 0)
                    if i:
                        dve.wait_ge(s_g3d, i)
                        nc.vector.scalar_tensor_tensor(yo[0:n, t, :], yo[0:n, t, :], rstd[0:n, t, 1:2],
                                                       g3[0:n, 1, :], ALU.mult, ALU.add).then_inc(s_yo, 1)

            dve.wait_ge(s_kr, NS)
            sc4 = ssc[:, 0:2 * NS * H].rearrange("p (c b h) -> p c b h", c=2, b=NS)
            for c in range(2):
                nc.vector.tensor_tensor(sc4[:, c], sc4[:, c], bsm[:, c, :].unsqueeze(1).broadcast_to((P, NS, H)),
                                        ALU.add).then_inc(s_ss, 1)
            sample_softmax(0, H)
            sample_pick(0)
            residual(32)
            layer_norm(0)

            rows_out(7, qs_nat[0:NS, :], NS, D)
            def mem_head_max(h):
                b = h % 2
                dve.wait_ge(s_sc, h + 1)
                link(nc.vector.tensor_reduce(mx[:, b, :], ps[:, 4 + b, :].rearrange("p (c m) -> p c m", c=2), AX.X,
                                             ALU.max))
                dve.wait_ge(s_pt, h - 1)
                nc.vector.tensor_scalar(nm[:, b, :], mx[:, b, :], -1.0, None, ALU.mult).then_inc(s_nm, 1)

            mem_parts = ((0, 256), (256, 512))
            mem_head_max(H)
            for h in range(H, H + MH):
                head_norm(h, mem_parts)
                if h + 1 < H + MH:
                    mem_head_max(h + 1)
                if h > H:
                    key_scores(BY_DVE[h - H - 1])
            for b in BY_DVE[MH - 1:]:
                key_scores(b)
            for b in BY_POOL:
                if b not in BY_ACT:
                    key_sums("mk", D, MH, b, NS + BY_POOL.index(b) + 1, s_kr2)
            sample_softmax(1, MH)
            sample_pick(1)
            residual(48)
            layer_norm(1)

            dve.wait_ge(s_kvst, 64)
            for tl in (lgt, posm, gat, SelT, yb):
                ins = nc.vector.memset(tl, 0.0)
                if tl is not yb:
                    own[0] += 1
                    ins.then_inc(dve_own, 1)
            ins.then_inc(s_yz, 1)
            dve.wait_ge(dve_own, own[0])
            dve.wait_ge(s_rt, 1)
            nc.vector.tensor_scalar(lgTs[0:NX, :], ps[0:NX, 0, 0:T], brc[0:NX, :], None, ALU.add).then_inc(
                s_rt_out, 1)
            dve.wait_ge(s_rt, 2)
            own[0] += 2
            nc.vector.tensor_copy(lgt[:, 0:2, :], ps[:, 1, 0:2 * NX].rearrange("p (t e) -> p t e", t=2)).then_inc(
                dve_own, 1)
            nc.vector.tensor_copy(lgt[0:NS, 2, :], ps[0:NS, 1, 2 * NX:3 * NX]).then_inc(dve_own, 1)
            dve.wait_ge(dve_own, own[0])
            for t in range(3):
                own[0] += 1
                nc.vector.max(top8[:, t, :], lgt[:, t, :]).then_inc(dve_own, 1)
            dve.wait_ge(dve_own, own[0])
            wide = lambda v: v.broadcast_to((P, 3, NX))
            own[0] += 2
            nc.vector.tensor_tensor(gtm, lgt, wide(top8[:, :, 3:4]), ALU.is_gt).then_inc(dve_own, 1)
            nc.vector.tensor_tensor(eqm, lgt, wide(top8[:, :, 3:4]), ALU.is_equal).then_inc(dve_own, 1)
            dve.wait_ge(dve_own, own[0])
            link(nc.vector.tensor_reduce(left, gtm, AX.X, ALU.add))
            for t in range(3):
                own[0] += 1
                nc.vector.tensor_tensor_scan(cum[:, t, :], con("ones")[:, 0:NX], eqm[:, t, :], left[:, t:t + 1],
                                             ALU.mult, ALU.add).then_inc(dve_own, 1)
            dve.wait_ge(dve_own, own[0])
            link(nc.vector.scalar_tensor_tensor(cum, cum, float(TOPK), eqm, ALU.is_le, ALU.mult))
            nc.vector.tensor_tensor(msk, cum, gtm, ALU.add).then_inc(s_rt_out, 1)
            nc.vector.tensor_tensor(rex, lgt, wide(top8[:, :, 0:1]), ALU.subtract).then_inc(s_rt_out, 1)
            dve.wait_ge(s_rt_out, 2)
            dve.wait_ge(s_rt, 3)
            own[0] += 2
            nc.vector.scalar_tensor_tensor(posm[:, 0:2, :], ps[:, 1, 128:192].rearrange("p (t e) -> p t e", t=2),
                                           1.0, msk[:, 0:2, :], ALU.add, ALU.mult).then_inc(dve_own, 1)
            nc.vector.scalar_tensor_tensor(posm[0:NS, 2:3, :], ps[0:NS, 1, 192:224].unsqueeze(1), 1.0,
                                           msk[0:NS, 2:3, :], ALU.add, ALU.mult).then_inc(dve_own, 1)
            dve.wait_ge(dve_own, own[0])

            four = (P, 3, 2, SLOTS)
            iota4 = con("iota").rearrange("p (a s) -> p a s", a=2).unsqueeze(1).broadcast_to(four)

            def select(q):
                nc.vector.tensor_tensor(Sel, iota4, posm[:, :, bass.ds(q, 2)].unsqueeze(3).broadcast_to(four),
                                        ALU.is_equal).then_inc(e_sel, 1)

            def pick_biases(q):
                nc.vector.tensor_copy(selE, ident[:, bass.ds(q, 2)].unsqueeze(2).broadcast_to((P, 2, SLOTS))
                                      ).then_inc(e_sb, 1)

            def advance(q, n):
                dve.wait_ge(e_sel, n)
                nc.vector.tensor_tensor(SelG, Sel, gat[:, :, bass.ds(q, 2)].unsqueeze(3).broadcast_to(four),
                                        ALU.mult).then_inc(e_selg, 1)
                nc.vector.tensor_scalar(posm[:, :, bass.ds(q, 2)], posm[:, :, bass.ds(q, 2)], -float(SLOTS), None,
                                        ALU.add).then_inc(e_pos, 1)

            select(0)
            link(nc.vector.tensor_reduce(cmax[0:1, :], ps[0:1, 1, 224:256], AX.X, ALU.max))
            link(nc.vector.tensor_scalar(lim4[0:1, :], con("limit")[0:1, :], cmax[0:1, :], None, ALU.is_lt))
            link(nc.vector.tensor_reduce(over[0:1, :], lim4[0:1, :], AX.X, ALU.add))
            for i, (per, at0) in enumerate(((16.0, 16.0), (8.0, 8.0), (8.0, 7.0), (16.0, 15.0))):
                nc.vector.tensor_scalar(nswi[0:1, i:i + 1], over[0:1, :], per, at0, ALU.mult, ALU.add).then_inc(
                    s_nsw, 1)
            pick_biases(0)
            dve.wait_ge(s_gex, 1)
            link(nc.vector.tensor_tensor(rex, rex, msk, ALU.mult))
            link(nc.vector.tensor_reduce(rsum, rex, AX.X, ALU.add))
            link(nc.vector.reciprocal(rsum, rsum))
            nc.vector.tensor_tensor(gat, rex, wide(rsum.unsqueeze(2)), ALU.mult).then_inc(s_rt_out, 1)
            dve.wait_ge(s_rt_out, 4)
            advance(0, 1)
            dve.wait_ge(s_x2, 3)
            nc.vector.tensor_scalar(xT, xT, ALPHA, None, ALU.mult).then_inc(s_alpha, 1)
            dve.wait_ge(s_rt, 4)
            for half in range(2):
                nc.vector.tensor_copy(SelT[0:NX, half, :], ps[0:NX, 3, 0:T]).then_inc(s_rt_out, 1)

            def clamp(k):
                dve.wait_ge(e_gu, k + 1)
                nc.vector.tensor_scalar(g2, ps[:, 0, :], 7.0, None, ALU.min).then_inc(e_g2, 1)
                dve.wait_ge(e_act, k + 1)
                nc.vector.tensor_scalar(u2, ps[:, 1, :], 7.0, -7.0, ALU.min, ALU.max).then_inc(e_u2, 1)

            def swiglu(k):
                dve.wait_ge(e_u2, k + 2)
                nc.vector.scalar_tensor_tensor(u2, u2, 1.0, g2, ALU.add, ALU.mult).then_inc(e_mul, 1)
                dve.wait_ge(e_mul, k + 1)
                dve.wait_ge(e_sig, k + 1)
                dve.wait_ge(e_at, k + 1)
                nc.vector.tensor_tensor(act_, u2, sg_, ALU.mult).then_inc(e_act, 1)

            def add_scattered(n):
                dve.wait_ge(e_y_out, DC * n + 1)
                for c in range(DC):
                    dve.wait_ge(e_y, DC * n + (c + 1))
                    nc.vector.tensor_tensor(xT[:, c, :], xT[:, c, :], ps[:, 2 + c % 2, 0:T], ALU.add).then_inc(
                        e_y_out, 1)

            dve.wait_ge(s_alpha, 1)
            for first in (e_u2, e_st_out, e_act, e_y_out):
                dve.sem_inc(first, 1)
            pairs = dve.value_load(nswi[0:1, 0:1], min_val=16, max_val=80)
            with dve.Fori(0, pairs) as it:
                clamp(2 * it)
                swiglu(2 * it)
                add_scattered(it)
                dve.wait_ge(e_st, it + 1)
                nc.vector.tensor_copy(SelT[:, 0, :], ps[:, 3, 0:T]).then_inc(e_st_out, 1)
                nc.vector.tensor_copy(SelT[0:64, 1, :], ps[64:P, 3, 0:T]).then_inc(e_st_out, 1)
                nc.vector.tensor_copy(SelT[64:P, 1, :], ps[0:64, 3, 0:T]).then_inc(e_st_out, 1)
                q = ((it + 1) % 16) * 2
                dve.wait_ge(e_pos, it + 1)
                dve.wait_ge(e_selg, it + 1)
                select(q)
                advance(q, it + 2)
                clamp(2 * it + 1)
                pick_biases(q)
                swiglu(2 * it + 1)
            dve.wait_ge(e_dn, 2 * pairs)
            nc.vector.tensor_copy(yb[:, 1, :], ps[:, 5, :]).then_inc(s_yb_last, 1)
            last_layer_norm()

        @block.tensor
        def _(pe):
            mm = nc.tensor.matmul
            tp = nc.tensor.transpose
            pe.wait_ge(s_ident, 32)
            x2 = halves(("xp", 0))
            for c in range(DC):
                if c % 4 == 0:
                    pe.wait_ge(landed[0] if c else s_x0, 16)
                if c >= 4:
                    pe.wait_ge(s_xT_out, c - 3)
                cols = slice(P * c, P * c + P)
                tp(ps[:, c % 4, 0:P], x2[:, 0, cols], ident)
                tp(ps[:, c % 4, P:2 * P], x2[:, 1, cols], ident)
                tp(ps[:, c % 4, NP_:T], xh[0:NS, 2, cols], ident[0:NS, 0:NS]).then_inc(s_xT, 1)
            arrived(pe, ("mp", 0))
            m2_ = halves(("mp", 0))
            for c in range(DC):
                if c >= 4:
                    pe.wait_ge(s_mT_out, c - 3)
                tp(ps[:, 4 + c % 4, 0:P], m2_[:, 0, P * c:P * c + P], ident)
                tp(ps[:, 4 + c % 4, P:2 * P], m2_[:, 1, P * c:P * c + P], ident).then_inc(s_mT, 1)
            pe.wait_ge(s_mT_out, DC)
            pe.wait_ge(s_const, 48)
            pe.wait_ge(s_zero, 3)
            oh = con("oh")[0:NX + 1, :]
            tb = tab[0:NX + 1, :]
            mm(ps[0:H, 4, 0:384], tb, oh[:, 0:384], start=True, stop=True)
            for c in range(2):
                mm(ps[:, 5, c * H:(c + 1) * H], oh[:, 384 + c * P:384 + (c + 1) * P], tb, start=True, stop=True)
            mm(ps[0:NS * H, 5, 32:33], tab8[0:NX + 1, :], oh[:, 640:641], start=True, stop=True)
            for c in range(2):
                ins = tp(ps[:, 6, 16 * c:16 * c + 16], xh[0:2 * NS, 0, P * c:P * c + P], ident[0:2 * NS, 0:2 * NS])
            ins.then_inc(s_bt, 1)

            def stay_awake(n, out):
                for _ in range(n):
                    mm(out, ident, ident, start=True, stop=True)

            def dense_half(what, i, tiles):
                arrived(pe, (what, i))
                w = quarters((what, i))
                count = len(tiles)
                n0 = TILE0[what] + count * (i // 2)
                for j in range(count):
                    n = n0 + j
                    if i % 2 == 0 and n >= 4:
                        pe.wait_ge(s_dn_out, n - 3)
                    out, lhs, rhs = tiles[j]
                    for k in range(4):
                        kk = 4 * (i % 2) + k
                        ins = mm(out(n), lhs(w, k, kk), rhs(w, k, kk), start=(kk == 0), stop=(kk == 7))
                    if i % 2:
                        ins.then_inc(s_dn, 1)
                if i % 2 == 0:
                    ins.then_inc(s_half, 1)

            def columns(x):
                return [(lambda n: ps[:, n % 4, 0:T],
                         lambda w, k, kk, j=j: w[:, k, P * j:P * j + P],
                         lambda w, k, kk: x[:, kk, :]) for j in range(4)]

            def token_rows(x):
                return [(lambda n: ps[:, n % 4, :],
                         lambda w, k, kk, m=m: x[:, kk, P * m:P * m + P],
                         lambda w, k, kk: w[:, k, :]) for m in range(2)]

            def win_half(i):
                for p in (2 * i, 2 * i + 1):
                    pe.wait_ge(s_wlo, p + 1)
                    for j in range(4):
                        n = 4 * (i // 2) + j
                        if p % 4 == 0 and n >= 4:
                            pe.wait_ge(s_dn_out, n - 3)
                        for k in range(2):
                            kk = 2 * (p % 4) + k
                            cols = slice(512 * k + P * j, 512 * k + P * j + P)
                            terms = ((w_hi, x_hi), (w_hi, x_lo), (w_lo, x_hi))
                            for m, (w, x) in enumerate(terms):
                                ins = mm(ps[:, n % 4, 0:T], w[p % 2][:, cols], x[kk],
                                         start=(kk == 0 and m == 0), stop=(kk == 7 and m == 2))
                        if p % 4 == 3:
                            ins.then_inc(s_dn, 1)
                    if p % 4 < 3:
                        ins.then_inc(s_wused, 1)

            pe.wait_ge(s_xlo, DC)
            for i in range(6):
                win_half(i)

            def turn(k, src, col, n, chunks):
                b = (4, 4, 6, 4, 6, 4, 6)[k] if k < 7 else 4
                if k in (3, 4, 5, 6):
                    pe.wait_ge(s_nat_out, k - 1)
                for c in range(chunks):
                    ins = tp(psf[0:n, 512 * b + P * c:512 * b + P * c + P], src[:, c, col:col + n], ident)
                ins.then_inc(s_nat, 1)

            for i in range(6, 12):
                win_half(i)
                if i == 6:
                    pe.wait_ge(s_dn_out, 12)
                    pe.wait_ge(s_bt_out, 4)
                    turn(0, proj[:, Q0:K0, :], NP_, NS, HP)
            pe.wait_ge(s_dn_out, 24)
            pe.wait_ge(s_nat_out, 1)
            for k, (src, t) in enumerate([(V0, 0), (V0, 1), (V0, 2), (K0, 0), (K0, 1), (K0, 2)]):
                turn(k + 1, proj[:, src:src + HP, :], TCH[t][0], TCH[t][1], HP)

            def scores(h):
                r, c, b = E * (h % 2), h // 2, 4 + h % 2
                if h >= 2:
                    pe.wait_ge(s_nm, h - 1)
                q = proj[r:r + E, Q0 + c, :]
                k = proj[r:r + E, K0 + c, :]
                mm(ps[:, b, 0:P], q[:, 0:P], k[:, 0:P], start=True, stop=True)
                mm(ps[:, b, P:3 * P], q[:, P:2 * P], k[:, 0:2 * P], start=True, stop=True).then_inc(s_sc, 1)

            def probs_turned(h):
                pe.wait_ge(s_pn, 2 * h + 2)
                if h >= 1:
                    pe.wait_ge(s_pt_out, h)
                for j in range(3):
                    ins = tp(ps[:, 6, P * j:P * j + P], lg[:, h % 2, P * j:P * j + P], ident)
                ins.then_inc(s_pt, 1)

            def values(h):
                pe.wait_ge(s_pt_out, h + 1)
                if h >= 1:
                    pe.wait_ge(s_av_out, h)
                r = E * (h % 2)
                v = vnat[:, :, E * h:E * h + E]
                mm(ps[r:r + E, 7, 0:P], v[:, 0, :], pt[:, h % 2, 0:P], start=True, stop=True)
                mm(ps[r:r + E, 7, P:NP_], v[:, 0, :], pt[:, h % 2, P:NP_], start=True, stop=False)
                mm(ps[r:r + E, 7, P:NP_], v[:, 1, :], pt[:, h % 2, NP_:NP_ + P], start=False,
                   stop=True).then_inc(s_av, 1)

            pe.wait_ge(s_nat_out, 7)
            for step in range(H + 2):
                if step < H:
                    scores(step)
                if 1 <= step <= H:
                    probs_turned(step - 1)
                if step >= 2:
                    values(step - 2)
                f = FILL.get(step)
                if f is not None:
                    dense_half("wmv" if f < 4 else "wmk", f % 4, token_rows(memT))
            pe.wait_ge(s_dn_out, 32)
            for c in range(DC):
                if c == 0:
                    pe.wait_ge(s_av_out, H)
                if c >= 4:
                    pe.wait_ge(s_mkT_out, c - 3)
                for m in range(2):
                    ins = tp(ps[:, 4 + c % 4, P * m:P * m + P], memk_nat[:, m, P * c:P * c + P], ident)
                ins.then_inc(s_mkT, 1)

            def sample_attention(k, heads, vv, width):
                n = NS * heads
                if k == 0:
                    pe.wait_ge(s_mkT_out, DC)
                    pe.wait_ge(s_ss, 2)
                else:
                    pe.wait_ge(s_av_out, H + MH)
                    stay_awake(30, ps[:, 7, 0:P])
                    pe.wait_ge(s_kr2, NS - len(BY_ACT))
                    pe.wait_ge(s_ka, len(BY_ACT))
                for c in range(2):
                    ins = tp(ps[0:n, 4, P * c:P * c + P], ssc[:, n * c:n * c + n], ident)
                ins.then_inc(s_sT, 1)
                stay_awake(6, ps[:, 5, 0:P])
                pe.wait_ge(s_spn, k + 1)
                for c in range(2):
                    ins = tp(ps[:, 5, n * c:n * c + n], es[0:n, P * c:P * c + P], ident[0:n, 0:n])
                if k == 0:
                    ins = mm(ps[0:NS, 6, 0:n], es[0:n, 256:257].broadcast_to((n, NS)), ident[0:n, 0:n],
                             start=True, stop=True)
                ins.then_inc(s_spT, 1)
                pe.wait_ge(s_spT_out, 2 if k == 0 else 3)
                for g in range(2):
                    terms = [0, 1, 2] if k == 0 else [0, 1]
                    for a in range(0, width, 512):
                        z = min(a + 512, width)
                        for t in terms:
                            for lane in range(4):
                                b = 4 * g + lane
                                if a == 0 and t == 0:
                                    arrived(pe, (vv, b))
                                out = psf[32 * lane:32 * lane + 32, 2048 + 1024 * g + a:2048 + 1024 * g + z]
                                if t < 2:
                                    w = pts[:, t, heads * b:heads * b + 32]
                                    v = halves((vv, b))[:, t, a:z]
                                else:
                                    w = selfw[0:NS, heads * b:heads * b + 32]
                                    v = vs_nat[0:NS, a:z]
                                ins = mm(out, w, v, start=(t == 0), stop=(t == terms[-1]))
                    ins.then_inc(s_sav, 1)
                for g in range(2):
                    pe.wait_ge(s_sav_out, 2 * k + g + 1)
                    for c in range(width // P):
                        a = 2048 + 1024 * g + P * c
                        ins = tp(psf[:, a:a + P], avs[:, g, P * c:P * c + P], ident)
                    ins.then_inc(s_sat, 1)

            sample_attention(0, H, "wv", AW)
            pe.wait_ge(s_sat_out, 2 * H)
            for i in range(4):
                dense_half("wout", i, columns(mixT))

            def layer_norm(k):
                pe.wait_ge(s_dn_out, 40 if k == 0 else 56)
                for t, (t0, n) in enumerate(TCH):
                    b = ROWB[t]
                    for c in range(DC):
                        ins = tp(psf[0:n, 512 * b + P * c:512 * b + P * c + P], xT[:, c, t0:t0 + n], ident)
                    ins.then_inc(s_ln, 1)
                for t, (t0, n) in enumerate(TCH):
                    pe.wait_ge(s_xh, 3 * k + t + 1)
                    for c in range(4):
                        ins = tp(ps[:, 2 + c, t0:t0 + n], xh[0:n, t, P * c:P * c + P], ident[0:n, 0:n])
                        if t == 2:
                            ins.then_inc(s_lt, 1)
                    if t < 2:
                        stay_awake(4, ps[:, 2, 384:512])
                for c in range(4, DC):
                    pe.wait_ge(s_lt_odd if c % 2 else s_lt_out, 4 * k + (c - 4) // 2 + 1)
                    for t, (t0, n) in enumerate(TCH):
                        ins = tp(ps[:, 2 + c % 4, t0:t0 + n], xh[0:n, t, P * c:P * c + P], ident[0:n, 0:n])
                    ins.then_inc(s_lt, 1)
                pe.wait_ge(s_lt_out, 4 * k + 4)
                pe.wait_ge(s_lt_odd, 4 * k + 4)

            layer_norm(0)
            for i in range(4):
                dense_half("wmq", i, columns(xT))
            pe.wait_ge(s_dn_out, 48)
            turn(7, mqT, NP_, NS, DC)
            for h in range(H, H + MH + 2):
                j = h - H
                if j < MH:
                    if j >= 2:
                        pe.wait_ge(s_ex, 2 * h - 2)
                    if j == 0:
                        pe.wait_ge(s_nat_out, 8)
                    for qc in range(2):
                        for ec in range(2):
                            ins = mm(ps[:, 4 + h % 2, MT * qc:MT * qc + MT], mqT[:, 2 * j + ec, P * qc:P * qc + P],
                                     memkT[:, 2 * j + ec, :], start=(ec == 0), stop=(ec == 1))
                    ins.then_inc(s_sc, 1)
                if 1 <= j <= MH:
                    pe.wait_ge(s_pn, 2 * h)
                    pe.wait_ge(s_pt_out, h - 1)
                    for qc in range(2):
                        for mc in range(2):
                            ins = tp(ps[:, 6, MT * mc + P * qc:MT * mc + P * qc + P],
                                     lg[:, (h - 1) % 2, MT * qc + P * mc:MT * qc + P * mc + P], ident)
                    ins.then_inc(s_pt, 1)
                if j >= 2:
                    pe.wait_ge(s_pt_out, h - 1)
                    pe.wait_ge(s_av_out, h - 2)
                    for ec in range(2):
                        c0 = MT * (j - 2) + P * ec
                        for mc in range(2):
                            ins = mm(ps[:, 7, NP_ * ec:NP_ * ec + NP_], memv[:, mc, c0:c0 + P],
                                     pt[:, h % 2, MT * mc:MT * mc + MT], start=(mc == 0), stop=(mc == 1))
                    ins.then_inc(s_av, 1)
            sample_attention(1, MH, "mv", D)
            pe.wait_ge(s_sat_out, 2 * H + 2 * DC)
            for i in range(4):
                dense_half("wmo", i, columns(mixT))
            layer_norm(1)

            pe.wait_ge(s_late, 16)
            for c in range(DC):
                ins = mm(ps[0:NX, 0, 0:T], wr[:, c, :], xT[:, c, :], start=(c == 0), stop=(c == 7))
            ins.then_inc(s_rt, 1)

            def x2_rows(t):
                (t0, n), b = TCH[t], (4, 6, 2)[t]
                for c in range(DC):
                    ins = tp(psf[0:n, 512 * b + P * c:512 * b + P * c + P], xT[:, c, t0:t0 + n], ident)
                ins.then_inc(s_x2, 1)

            x2_rows(0)
            pe.wait_ge(s_rt_out, 1)
            for t, (t0, n) in enumerate(TCH):
                ins = tp(ps[0:n, 1, NX * t:NX * t + NX], lgTs[0:NX, t0:t0 + n], ident[0:NX, 0:NX])
            ins.then_inc(s_rt, 1)
            x2_rows(1)
            x2_rows(2)
            stay_awake(8, ps[:, 0, 384:512])
            pe.wait_ge(s_rt_out, 2)
            pe.wait_ge(s_low, 2)
            for t, (t0, n) in enumerate(TCH):
                for c in range(t + 1):
                    m = TCH[c][1]
                    w = (beforeb if c == t else onesb)[0:m, 0:n]
                    mm(ps[0:n, 1, 128 + NX * t:128 + NX * t + NX], w, msk[0:m, c, :], start=(c == 0), stop=(c == t))
            for c in range(3):
                m = TCH[c][1]
                ins = mm(ps[0:1, 1, 224:256], onesb[0:m, 0:1], msk[0:m, c, :], start=(c == 0), stop=(c == 2))
            ins.then_inc(s_rt, 1)

            def gather():
                for c in range(DC):
                    for t, (_, n) in enumerate(TCH):
                        ins = mm(ps[:, 6 + c // 4, P * (c % 4):P * (c % 4) + P], xh[0:n, t, P * c:P * c + P],
                                 Sel[0:n, t].rearrange("p a s -> p (a s)"), start=(t == 0), stop=(t == 2))
                ins.then_inc(e_gx, 1)

            pe.wait_ge(s_x2_out, 3)
            pe.wait_ge(e_sel, 1)
            gather()
            pe.wait_ge(s_rt_out, 4)
            for t, (t0, n) in enumerate(TCH):
                ins = tp(ps[0:NX, 3, t0:t0 + n], gat[0:n, t, :], ident[0:n, 0:n])
            ins.then_inc(s_rt, 1)
            pe.wait_ge(s_nsw, 4)

            def gate_up(r, k):
                a = k % 2
                for c in range(-1, 8):
                    if c >= 0:
                        item_arrived(pe, r, PER_EXPERT * k + c)
                        w, x = expert_slot(PER_EXPERT * k + c), xTe[:, c, SLOTS * a:SLOTS * a + SLOTS]
                    else:
                        w, x = bgu, selE[:, a, :]
                    for gu in range(2):
                        for j in range(2):
                            ins = mm(ps[64 * j:64 * j + 64, gu, :], x,
                                     w[:, D * gu + 512 * j:D * gu + 512 * j + 512], start=(c < 0), stop=(c == 7),
                                     skip_group_check=True)
                    if 0 <= c < 7:
                        ins.then_inc(e_wu, 1)
                ins.then_inc(e_gu, 1)

            def turn_act():
                for q in range(4):
                    ins = tp(ps[:, 2, P * q:P * q + P], act_[:, P * q:P * q + P], ident)
                ins.then_inc(e_at, 1)

            def down(r, k):
                for i in range(4):
                    item_arrived(pe, r, PER_EXPERT * k + 8 + i)
                    w = expert_slot(PER_EXPERT * k + 8 + i).rearrange("p (k n) -> p k n", k=2)
                    for kk in range(2):
                        m = 2 * i + kk
                        x = actT[:, m % 4, 64 * (m // 4):64 * (m // 4) + 64]
                        for j in range(2):
                            half = j if k % 2 == 0 else 1 - j
                            ins = mm(ps[64 * j:64 * j + 64, 4 + half, :], x, w[:, kk, 512 * half:512 * half + 512],
                                     start=(m == 0), stop=(m == 7), skip_group_check=True)
                    ins.then_inc(e_du if i < 3 else e_dn, 1)

            def scatter():
                for c in range(DC):
                    half = c // 4
                    if c >= 2:
                        pe.wait_ge(e_y_out, scattered[0] + c)
                    mm(ps[:, 2 + c % 2, 0:T], yb[:, half, P * (c % 4):P * (c % 4) + P], SelT[:, half, :],
                       start=True, stop=True).then_inc(e_y, 1)

            scattered = [0]
            pe.sem_inc(e_at, 1)
            pairs = pe.value_load(nswi[0:1, 0:1], min_val=16, max_val=80)
            last_round = pe.value_load(nswi[0:1, 2:3], min_val=7, max_val=39)
            pe.wait_ge(s_bgu, 16)

            def sum_turned(t, half):
                t0, n = TCH[t]
                for c in range(4 * half, 4 * half + 4):
                    a = 512 * LASTB[t] + P * c
                    mm(psf[0:n, a:a + P], xT[:, c, t0:t0 + n], ident, start=(c % 4 == 0), stop=False,
                       skip_group_check=True)

            def pair(r, j, last=False):
                it = 2 * r + j
                scattered[0] = DC * it
                pe.wait_ge(e_gx_out, it + 1)
                pe.wait_ge(e_sb, it + 1)
                pe.wait_ge(e_u2, 2 * it + 1)
                gate_up(r, 2 * j)
                pe.wait_ge(s_first, 16)
                pe.wait_ge(s_rt_out, 6)
                pe.wait_ge(s_alpha, 1)
                pe.wait_ge(e_yb, it + 1)
                pe.wait_ge(e_st_out, 3 * it + 1)
                pe.wait_ge(e_at_out, 2 * it + 1)
                scatter()
                pe.wait_ge(e_y_out, DC * it + (DC + 1))
                pe.wait_ge(e_selg, it + 1)
                for t, (t0, n) in enumerate(TCH):
                    ins = tp(ps[:, 3, t0:t0 + n], SelG[0:n, t].rearrange("p a s -> p (a s)"), ident[0:n, 0:n])
                ins.then_inc(e_st, 1)
                pe.wait_ge(e_act, 2 * it + 2)
                turn_act()
                pe.wait_ge(e_at_out, 2 * it + 2)
                down(r, 2 * j)
                if last:
                    sum_turned(0, 0)
                    sum_turned(0, 1)
                    pe.wait_ge(e_st_out, 3 * it + 4)
                    sum_turned(1, 1)
                pe.wait_ge(e_u2, 2 * it + 2)
                gate_up(r, 2 * j + 1)
                if last:
                    pe.wait_ge(e_u2, 2 * it + 3)
                    sum_turned(2, 0)
                    sum_turned(2, 1)
                else:
                    pe.wait_ge(e_sel, it + 2)
                    gather()
                pe.wait_ge(e_act, 2 * it + 3)
                turn_act()
                pe.wait_ge(e_at_out, 2 * it + 3)
                if last:
                    sum_turned(1, 0)
                down(r, 2 * j + 1)

            with pe.Fori(0, last_round) as r:
                for j in range(2):
                    pair(r, j)
            pair(last_round, 0)
            pair(last_round, 1, last=True)
            pe.wait_ge(e_yb, pairs + 1)
            pe.wait_ge(s_yb_last, 1)
            for t in LORDER:
                t0, n = TCH[t]
                for half in range(2):
                    ins = mm(ps[0:n, LASTB[t] + half, :], SelT[:, half, t0:t0 + n], yb[:, half, :], start=False,
                             stop=True, skip_group_check=True)
                ins.then_inc(s_ln, 1)


_INS = ["x_prompt", "x_sample", "mem_prompt", "cache_win_k", "cache_win_v", "state_conv", "cache_mem_k",
        "cache_mem_v", "rel_bias_table", "w_in", "w_conv", "w_out", "ln1_g", "ln1_b", "w_mem_q", "w_mem_k",
        "w_mem_v", "w_mem_o", "ln2_g", "ln2_b", "w_router", "b_router", "w_gate_up", "b_gate_up", "w_down",
        "b_down", "ln3_g", "ln3_b"]
_OUTS = [(1, NP_, D), (NS, 1, D), (1, 1, NP_, H, E), (1, 1, NP_, H, E), (1, 1, 2, CW), (1, 1, MT, MH, D // MH),
         (1, 1, MT, MH, D // MH), (1, NS, 1, H, E), (1, NS, 1, H, E), (1, NS, 2, CW)]


def kernel(**inputs):
    import numpy as _np
    import concourse.bacc as _bacc
    from concourse import mybir as _mybir
    from concourse.bass_utils import run_bass_kernel_spmd as _run

    nc = _bacc.Bacc("TRN2", target_bir_lowering=False, num_devices=1)
    arrays, args = {}, []
    for name in _INS:
        a = _np.ascontiguousarray(inputs[name])
        arrays[f"in_{name}_dram"] = a
        args.append(nc.dram_tensor(f"in_{name}_dram", a.shape, _mybir.dt.from_np(a.dtype), kind="ExternalInput").ap())
    arrays["shape_constants"] = CONST
    args.append(nc.dram_tensor("shape_constants", CONST.shape, _mybir.dt.float32, kind="ExternalInput").ap())
    for i, shape in enumerate(_OUTS):
        args.append(nc.dram_tensor(f"out_{i}_dram", shape, _mybir.dt.float32, kind="ExternalOutput").ap())
    decoder_layer(nc, *args)
    r = _run(nc, [arrays], core_ids=[0])
    return tuple(r.results[0][f"out_{i}_dram"] for i in range(len(_OUTS)))
```
